# Optimizing a Trainium2 kernel written in Bass

```python
import math
import jax, jax.numpy as jnp
from jax import lax
import numpy as np

D_MODEL = 1024
BATCH = 1
SEQ = 1024
DEPTH = 2

N_MIXERS = 2
HEAD_DIM = 64
ATTN_HEADS = D_MODEL // HEAD_DIM
ATTN_WIDTH = ATTN_HEADS * HEAD_DIM
DILATED_GROUPS = ((128, 1), (512, 4), (2048, 16))
N_GROUPS_A = len(DILATED_GROUPS)
ATTN_IN_COLS = 3 * N_GROUPS_A * ATTN_WIDTH + ATTN_WIDTH
REL_BUCKETS = 32
REL_MAX_DIST = 2048
SSM_WIDTH = D_MODEL
SSM_GROUP = 16
SSM_N_GROUPS = SSM_WIDTH // SSM_GROUP
SSM_STATE = 64
N_ATTN_LAYERS = (DEPTH + 1) // 2
N_SSM_LAYERS = DEPTH // 2
EPS = 1e-6
NEG = -1e30


def rms_norm(x, g):
    xf = x.astype(jnp.float32)
    y = xf * lax.rsqrt(jnp.mean(xf * xf, axis=-1, keepdims=True) + EPS) * g.astype(jnp.float32)
    return y.astype(x.dtype)

def t5_bucket(dist):
    max_exact = REL_BUCKETS // 2
    n = jnp.maximum(dist, 1).astype(jnp.float32)
    large = max_exact + (jnp.log(n / max_exact) / math.log(REL_MAX_DIST / max_exact)
                         * (REL_BUCKETS - max_exact)).astype(jnp.int32)
    large = jnp.minimum(large, REL_BUCKETS - 1)
    return jnp.where(dist < max_exact, dist, large)

def dilated_group_attention(q, k, v, rel_bias, window, dilation):
    B, S, H, E = q.shape
    steps = window // dilation
    blk = steps
    L = S // dilation
    nb = -(-L // blk)
    Lp = nb * blk

    def to_sub(t):
        t = t.reshape(B, L, dilation, H, E)
        return jnp.pad(t, ((0, 0), (0, Lp - L), (0, 0), (0, 0), (0, 0)))

    qs = to_sub(q).reshape(B, nb, blk, dilation, H, E)
    front = ((0, 0), (blk, 0), (0, 0), (0, 0), (0, 0))
    ks = jnp.pad(to_sub(k), front).reshape(B, nb + 1, blk, dilation, H, E)
    vs = jnp.pad(to_sub(v), front).reshape(B, nb + 1, blk, dilation, H, E)
    kw = jnp.concatenate([ks[:, :-1], ks[:, 1:]], axis=2)
    vw = jnp.concatenate([vs[:, :-1], vs[:, 1:]], axis=2)

    i = jnp.arange(blk)[:, None]
    j = jnp.arange(2 * blk)[None, :]
    back = blk + i - j
    band = (back >= 0) & (back <= steps)
    valid = band[None] & ((jnp.arange(nb)[:, None, None] > 0) | (j[None] >= blk))
    bias = rel_bias[t5_bucket(jnp.maximum(back, 0) * dilation)]
    bias = jnp.transpose(bias, (2, 0, 1)).astype(jnp.float32)

    scale = HEAD_DIM ** -0.5
    logits = jnp.einsum('bnqrhe,bnkrhe->bnrhqk', qs, kw,
                        preferred_element_type=jnp.float32) * scale + bias
    logits = jnp.where(valid[None, :, None, None], logits, NEG)
    lse = jax.nn.logsumexp(logits, axis=-1)
    p = jnp.exp(logits - lse[..., None])
    o = jnp.einsum('bnrhqk,bnkrhe->bnqrhe', p.astype(v.dtype), vw)
    o = o.reshape(B, Lp, dilation, H, E)[:, :L].reshape(B, S, H, E)
    lse = jnp.transpose(lse, (0, 1, 4, 2, 3)).reshape(B, Lp, dilation, H)[:, :L].reshape(B, S, H)
    return o, lse

def dilated_attention_mixer(h, w_in, w_out, rel_bias):
    B, S, _ = h.shape
    proj = h @ w_in
    n_qkv = 3 * N_GROUPS_A * ATTN_WIDTH
    qkv = proj[..., :n_qkv].reshape(B, S, 3, N_GROUPS_A, ATTN_HEADS, HEAD_DIM)
    z = proj[..., n_qkv:]
    outs, lses = [], []
    for g, (window, dilation) in enumerate(DILATED_GROUPS):
        o, l = dilated_group_attention(qkv[:, :, 0, g], qkv[:, :, 1, g], qkv[:, :, 2, g],
                                       rel_bias, window, dilation)
        outs.append(o)
        lses.append(l)
    wts = jax.nn.softmax(jnp.stack(lses), axis=0)
    o = jnp.sum(wts[..., None] * jnp.stack(outs).astype(jnp.float32), axis=0)
    o = o.reshape(B, S, ATTN_WIDTH).astype(h.dtype)
    return (o * jax.nn.silu(z)) @ w_out

def s5_scan(u, a_re, a_im, log_dt, b_re, b_im, c_re, c_im, d_skip):
    B, S, _ = u.shape
    f = jnp.float32
    uf = u.astype(f).reshape(B, S, SSM_N_GROUPS, SSM_GROUP)
    A = lax.complex(a_re.astype(f), a_im.astype(f))
    dt = jnp.exp(log_dt.astype(f))[:, None]
    a_bar = jnp.exp(A * dt)
    Bm = lax.complex(b_re.astype(f), b_im.astype(f))
    b_bar = ((a_bar - 1.0) / A)[..., None] * Bm
    bu = jnp.einsum('bsgc,gpc->bsgp', uf.astype(jnp.complex64), b_bar)
    a_elems = jnp.broadcast_to(a_bar, bu.shape)

    def combine(left, right):
        return (right[0] * left[0], right[0] * left[1] + right[1])

    _, states = lax.associative_scan(combine, (a_elems, bu), axis=1)
    Cm = lax.complex(c_re.astype(f), c_im.astype(f))
    y = jnp.einsum('bsgp,gcp->bsgc', states, Cm).real
    y = y + d_skip.astype(f).reshape(SSM_N_GROUPS, SSM_GROUP) * uf
    return y.reshape(B, S, SSM_WIDTH).astype(u.dtype)

def s5_mixer(h, w_in, a_re, a_im, log_dt, b_re, b_im, c_re, c_im, d_skip, w_glu, b_glu, w_out):
    proj = h @ w_in
    u, z = proj[..., :SSM_WIDTH], proj[..., SSM_WIDTH:]
    y = s5_scan(u, a_re, a_im, log_dt, b_re, b_im, c_re, c_im, d_skip)
    g = jax.nn.gelu(y)
    y = g * jax.nn.sigmoid(g @ w_glu + b_glu)
    return (y * jax.nn.silu(z)) @ w_out

def first_inputs(seed: int = 0) -> dict:
    key = jax.random.key(seed)
    ks = jax.random.split(key, 24)
    nrm = jax.random.normal
    f = jnp.float32
    NA, NS, D = N_ATTN_LAYERS, N_SSM_LAYERS, D_MODEL
    G, P, C, E = SSM_N_GROUPS, SSM_STATE, SSM_GROUP, SSM_WIDTH
    x = nrm(ks[0], (BATCH, SEQ, D), f)
    rel_bias = 0.5 * nrm(ks[1], (REL_BUCKETS, ATTN_HEADS), f)
    attn_pre_norm = 1.0 + 0.05 * nrm(ks[2], (NA, D), f)
    attn_w_in = nrm(ks[3], (NA, D, ATTN_IN_COLS), f) * D ** -0.5
    attn_w_out = nrm(ks[4], (NA, ATTN_WIDTH, D), f) * ATTN_WIDTH ** -0.5
    attn_post_norm = 1.0 + 0.05 * nrm(ks[5], (NA, D), f)
    ssm_pre_norm = 1.0 + 0.05 * nrm(ks[6], (NS, D), f)
    ssm_w_in = nrm(ks[7], (NS, D, 2 * E), f) * D ** -0.5
    ssm_a_re = -0.5 + 0.01 * nrm(ks[8], (NS, G, P), f)
    ssm_a_im = math.pi * jnp.arange(P, dtype=f)[None, None, :] + 0.01 * nrm(ks[9], (NS, G, P), f)
    ssm_log_dt = jax.random.uniform(ks[10], (NS, G), f, math.log(1e-3), math.log(1e-1))
    ssm_b_re = nrm(ks[11], (NS, G, P, C), f) * (2 * C) ** -0.5
    ssm_b_im = nrm(ks[12], (NS, G, P, C), f) * (2 * C) ** -0.5
    ssm_c_re = nrm(ks[13], (NS, G, C, P), f) * (2 * P) ** -0.5
    ssm_c_im = nrm(ks[14], (NS, G, C, P), f) * (2 * P) ** -0.5
    ssm_d = nrm(ks[15], (NS, E), f)
    ssm_w_glu = nrm(ks[16], (NS, E, E), f) * E ** -0.5
    ssm_b_glu = 0.02 * nrm(ks[17], (NS, E), f)
    ssm_w_out = nrm(ks[18], (NS, E, D), f) * E ** -0.5
    ssm_post_norm = 1.0 + 0.05 * nrm(ks[19], (NS, D), f)
    return {"x": x, "rel_bias": rel_bias,
            "attn_pre_norm": attn_pre_norm, "attn_w_in": attn_w_in,
            "attn_w_out": attn_w_out, "attn_post_norm": attn_post_norm,
            "ssm_pre_norm": ssm_pre_norm, "ssm_w_in": ssm_w_in,
            "ssm_a_re": ssm_a_re, "ssm_a_im": ssm_a_im, "ssm_log_dt": ssm_log_dt,
            "ssm_b_re": ssm_b_re, "ssm_b_im": ssm_b_im,
            "ssm_c_re": ssm_c_re, "ssm_c_im": ssm_c_im, "ssm_d": ssm_d,
            "ssm_w_glu": ssm_w_glu, "ssm_b_glu": ssm_b_glu,
            "ssm_w_out": ssm_w_out, "ssm_post_norm": ssm_post_norm}

def first_block(x, rel_bias, attn_pre_norm, attn_w_in, attn_w_out, attn_post_norm,
              ssm_pre_norm, ssm_w_in, ssm_a_re, ssm_a_im, ssm_log_dt,
              ssm_b_re, ssm_b_im, ssm_c_re, ssm_c_im, ssm_d,
              ssm_w_glu, ssm_b_glu, ssm_w_out, ssm_post_norm):
    for i in range(DEPTH):
        j = i // N_MIXERS
        if i % N_MIXERS == 0:
            h = rms_norm(x, attn_pre_norm[j])
            h = dilated_attention_mixer(h, attn_w_in[j], attn_w_out[j], rel_bias)
            x = x + rms_norm(h, attn_post_norm[j])
        else:
            h = rms_norm(x, ssm_pre_norm[j])
            h = s5_mixer(h, ssm_w_in[j], ssm_a_re[j], ssm_a_im[j], ssm_log_dt[j],
                         ssm_b_re[j], ssm_b_im[j], ssm_c_re[j], ssm_c_im[j], ssm_d[j],
                         ssm_w_glu[j], ssm_b_glu[j], ssm_w_out[j])
            x = x + rms_norm(h, ssm_post_norm[j])
    return x


GRID_W = 64
CTX_LEN = 256
CONV_W = 256
CONV_GROUPS = 4
CONV_K = 3
RET_HEADS = 6
RET_W = RET_HEADS * HEAD_DIM
NA_HEADS = 6
NA_W = NA_HEADS * HEAD_DIM
MIX_W = CONV_W + RET_W + NA_W
RET_CHUNK = 128
WIN_H = 8
WIN_W = 16
ROPE_BASE = 10000.0
LN_EPS = 1e-5
DEEPNORM_ALPHA = (2 * DEPTH) ** 0.25
DEEPNORM_BETA = (8 * DEPTH) ** -0.25

PROJ_SPLITS = (RET_W, RET_W, NA_W, NA_W,
               RET_W, RET_W, NA_W, NA_W,
               CONV_W, CONV_W, CONV_W, CONV_W)
PROJ_W = sum(PROJ_SPLITS)
KV_W = 2 * RET_W + 2 * NA_W


F32 = jnp.float32

def split_cols(p, sizes):
    idx = np.cumsum(sizes)[:-1].tolist()
    return jnp.split(p, idx, axis=-1)

def to_heads(t, n_heads):
    b, l, _ = t.shape
    return t.reshape(b, l, n_heads, HEAD_DIM).transpose(0, 2, 1, 3)

def from_heads(t):
    b, h, l, d = t.shape
    return t.transpose(0, 2, 1, 3).reshape(b, l, h * d)

def layer_norm(x, g, b):
    xf = x.astype(F32)
    mu = jnp.mean(xf, axis=-1, keepdims=True)
    var = jnp.mean(jnp.square(xf - mu), axis=-1, keepdims=True)
    return ((xf - mu) * lax.rsqrt(var + LN_EPS) * g + b).astype(x.dtype)

def head_norm(o):
    of = o.astype(F32)
    mu = jnp.mean(of, axis=-1, keepdims=True)
    var = jnp.mean(jnp.square(of - mu), axis=-1, keepdims=True)
    return (of - mu) * lax.rsqrt(var + LN_EPS)

def axial_rope_angles(n):
    t = jnp.arange(n)
    row = (t // GRID_W).astype(F32)
    col = (t % GRID_W).astype(F32)
    nf = HEAD_DIM // 4
    inv = ROPE_BASE ** (-jnp.arange(nf, dtype=F32) / nf)
    return row[:, None] * inv, col[:, None] * inv

def rotate(xp, ang):
    a, b = jnp.split(xp, 2, axis=-1)
    cos, sin = jnp.cos(ang), jnp.sin(ang)
    return jnp.concatenate([a * cos - b * sin, a * sin + b * cos], axis=-1)

def apply_axial_rope(x, ang_r, ang_c):
    xr, xc = jnp.split(x, 2, axis=-1)
    return jnp.concatenate([rotate(xr, ang_r), rotate(xc, ang_c)], axis=-1).astype(x.dtype)

def short_conv_branch(h, bg, cg, z, w, b):
    u = cg * h
    up = jnp.pad(u, ((0, 0), (1, 1), (0, 0)))
    conv = up[:, :-2] * w[0] + up[:, 1:-1] * w[1] + up[:, 2:] * w[2] + b
    return bg * conv * jax.nn.silu(z)

def ret_final_state(k, v, lg):
    l = k.shape[2]
    w = jnp.exp((l - 1 - jnp.arange(l, dtype=F32))[None, :] * lg[:, None])
    return jnp.einsum('bhld,hl,bhle->bhde', k, w, v)

def chunk_retention(q, k, v, lg, s0, inclusive):
    b, h, l, dk = q.shape
    dv = v.shape[-1]
    c = min(RET_CHUNK, l)
    nc = l // c
    qc = q.reshape(b, h, nc, c, dk)
    kc = k.reshape(b, h, nc, c, dk)
    vc = v.reshape(b, h, nc, c, dv)
    i = jnp.arange(c, dtype=F32)
    diff = i[:, None] - i[None, :]
    mask = diff >= 0 if inclusive else diff > 0
    dmat = jnp.where(mask[None], jnp.exp(jnp.where(mask, diff, 0.0)[None] * lg[:, None, None]), 0.0)
    scores = jnp.einsum('bhnid,bhnjd->bhnij', qc, kc) * dmat[None, :, None]
    o_inner = jnp.einsum('bhnij,bhnje->bhnie', scores, vc)
    wk = jnp.exp((c - 1 - i)[None, :] * lg[:, None])
    u = jnp.einsum('bhnjd,hj,bhnje->bhnde', kc, wk, vc)
    g_chunk = jnp.exp(c * lg)[:, None, None]

    def step(s, u_n):
        return g_chunk * s + u_n, s

    _, s_prev = lax.scan(step, s0, jnp.moveaxis(u, 2, 0))
    s_prev = jnp.moveaxis(s_prev, 0, 2)
    wq = jnp.exp((i + 1)[None, :] * lg[:, None])
    o_cross = jnp.einsum('bhnid,hi,bhnde->bhnie', qc, wq, s_prev)
    return (o_inner + o_cross).reshape(b, h, l, dv)

def bidir_retention(q, k, v, lg_f, lg_b, s_f, s_b):
    fwd = chunk_retention(q, k, v, lg_f, s_f, True)
    bwd = chunk_retention(jnp.flip(q, 2), jnp.flip(k, 2), jnp.flip(v, 2), lg_b, s_b, False)
    return fwd + jnp.flip(bwd, 2)

def retention_branch(q, k, v, g, kc, vc, qc, gc, decay_logit, need_ctx):
    n = q.shape[1]
    kscale = HEAD_DIM ** -0.5
    ang_r, ang_c = axial_rope_angles(n)
    qh = apply_axial_rope(to_heads(q, RET_HEADS), ang_r, ang_c)
    kh = apply_axial_rope(to_heads(k, RET_HEADS), ang_r, ang_c) * kscale
    vh = to_heads(v, RET_HEADS)
    kch = to_heads(kc, RET_HEADS) * kscale
    vch = to_heads(vc, RET_HEADS)
    lg = jax.nn.log_sigmoid(decay_logit.astype(F32))
    lg_f, lg_b = lg[0], lg[1]
    s_f = ret_final_state(kch, vch, lg_f)
    s_b = ret_final_state(jnp.flip(kch, 2), jnp.flip(vch, 2), lg_b)
    o = bidir_retention(qh, kh, vh, lg_f, lg_b, s_f, s_b)
    y = from_heads(head_norm(o)) * jax.nn.silu(g)
    if not need_ctx:
        return y, None
    qch = to_heads(qc, RET_HEADS)
    zero = jnp.zeros_like(s_f)
    oc = bidir_retention(qch, kch, vch, lg_f, lg_b, zero, zero)
    yc = from_heads(head_norm(oc)) * jax.nn.silu(gc)
    return y, yc

def neighbourhood_branch(q, k, v, g, kc, vc, qc, gc, rpb, need_ctx):
    b, n, _ = q.shape
    rows = n // GRID_W
    win_h = min(WIN_H, rows)
    n_loc = win_h * WIN_W
    scale = HEAD_DIM ** -0.5

    def grid(t):
        return to_heads(t, NA_HEADS).reshape(b, NA_HEADS, rows, GRID_W, HEAD_DIM)

    qg, kg, vg = grid(q), grid(k), grid(v)
    kch, vch = to_heads(kc, NA_HEADS), to_heads(vc, NA_HEADS)
    r = np.arange(rows)
    row_start = np.clip(r - win_h // 2, 0, rows - win_h)
    d_row = row_start[:, None] + np.arange(win_h)[None, :] - r[:, None]
    cpos = np.arange(GRID_W)
    col_idx = np.clip(cpos - WIN_W // 2, 0, GRID_W - WIN_W)[:, None] + np.arange(WIN_W)[None, :]
    d_col = col_idx - cpos[:, None]

    def row_block(args):
        q_r, rs, dr = args
        k_band = lax.dynamic_slice_in_dim(kg, rs, win_h, axis=2)
        v_band = lax.dynamic_slice_in_dim(vg, rs, win_h, axis=2)
        k_win = k_band[:, :, :, col_idx]
        v_win = v_band[:, :, :, col_idx]
        s_loc = jnp.einsum('bhcd,bhrckd->bhcrk', q_r, k_win).astype(F32) * scale
        bias = rpb[:, dr[:, None, None] + (WIN_H - 1), d_col[None] + (WIN_W - 1)]
        s_loc = s_loc + bias.transpose(0, 2, 1, 3)[None].astype(F32)
        s_ctx = jnp.einsum('bhcd,bhjd->bhcj', q_r, kch).astype(F32) * scale
        p = jax.nn.softmax(jnp.concatenate([s_loc.reshape(b, NA_HEADS, GRID_W, n_loc), s_ctx], axis=-1), axis=-1)
        p_loc = p[..., :n_loc].reshape(b, NA_HEADS, GRID_W, win_h, WIN_W).astype(v.dtype)
        p_ctx = p[..., n_loc:].astype(v.dtype)
        return (jnp.einsum('bhcrk,bhrckd->bhcd', p_loc, v_win)
                + jnp.einsum('bhcj,bhjd->bhcd', p_ctx, vch))

    o = lax.map(row_block, (jnp.moveaxis(qg, 2, 0),
                            jnp.asarray(row_start, jnp.int32),
                            jnp.asarray(d_row, jnp.int32)))
    y = o.transpose(1, 0, 3, 2, 4).reshape(b, n, NA_W) * jax.nn.silu(g)
    if not need_ctx:
        return y, None
    qch = to_heads(qc, NA_HEADS)
    s = jnp.einsum('bhid,bhjd->bhij', qch, kch).astype(F32) * scale
    oc = jnp.einsum('bhij,bhjd->bhid', jax.nn.softmax(s, axis=-1).astype(vc.dtype), vch)
    yc = from_heads(oc) * jax.nn.silu(gc)
    return y, yc

def hybrid_layer(x, xc, c_act, cc_act, w_mod, b_mod, w_in, conv_w, conv_b,
                 ret_decay, na_rpb, w_out, ln_g, ln_b, need_ctx):
    shift, scale, gate = jnp.split(c_act @ w_mod + b_mod, 3, axis=-1)
    h = x * (1 + scale[:, None]) + shift[:, None]
    rk, rv, nk, nv, rq, rg, nq, ng, ch, cb, ccg, cz = split_cols(h @ w_in, PROJ_SPLITS)
    n_mod = 3 if need_ctx else 2
    mod_c = jnp.split(cc_act @ w_mod[:, :n_mod * D_MODEL] + b_mod[:n_mod * D_MODEL], n_mod)
    hc = xc * (1 + mod_c[1]) + mod_c[0]
    if need_ctx:
        pc = split_cols(hc @ w_in, PROJ_SPLITS)
    else:
        pc = split_cols(hc @ w_in[:, :KV_W], PROJ_SPLITS[:4]) + [None] * 8
    rkc, rvc, nkc, nvc, rqc, rgc, nqc, ngc, chc, cbc, ccc, czc = pc

    y_conv = short_conv_branch(ch, cb, ccg, cz, conv_w, conv_b)
    y_ret, yc_ret = retention_branch(rq, rk, rv, rg, rkc, rvc, rqc, rgc, ret_decay, need_ctx)
    y_na, yc_na = neighbourhood_branch(nq, nk, nv, ng, nkc, nvc, nqc, ngc, na_rpb, need_ctx)
    y = jnp.concatenate([y_conv, y_ret, y_na], axis=-1) @ w_out
    x_new = layer_norm(DEEPNORM_ALPHA * x + gate[:, None] * y, ln_g, ln_b)
    if not need_ctx:
        return x_new, None
    yc_conv = short_conv_branch(chc, cbc, ccc, czc, conv_w, conv_b)
    yc = jnp.concatenate([yc_conv, yc_ret, yc_na], axis=-1) @ w_out
    xc_new = layer_norm(DEEPNORM_ALPHA * xc + mod_c[2] * yc, ln_g, ln_b)
    return x_new, xc_new

def second_inputs(seed: int = 0) -> dict:
    key = jax.random.key(seed)
    ks = jax.random.split(key, 14)
    nrm = jax.random.normal
    x = nrm(ks[0], (BATCH, SEQ, D_MODEL), F32)
    c = nrm(ks[1], (BATCH, D_MODEL), F32)
    ctx = nrm(ks[2], (BATCH, CTX_LEN, D_MODEL), F32)
    c_ctx = nrm(ks[3], (D_MODEL,), F32)
    w_mod = nrm(ks[4], (DEPTH, D_MODEL, 3 * D_MODEL), F32) * (0.5 * D_MODEL ** -0.5)
    b_mod = 0.01 * nrm(ks[5], (DEPTH, 3 * D_MODEL), F32)
    w_in = nrm(ks[6], (DEPTH, D_MODEL, PROJ_W), F32) * (D_MODEL ** -0.5)
    conv_w = nrm(ks[7], (DEPTH, CONV_K, CONV_W), F32) * (CONV_K ** -0.5)
    conv_b = 0.01 * nrm(ks[8], (DEPTH, CONV_W), F32)
    gamma = 1.0 - 2.0 ** (-5.0 - np.arange(RET_HEADS))
    decay_init = np.log(gamma / (1.0 - gamma)).astype(np.float32)
    ret_decay = jnp.asarray(decay_init)[None, None, :] + 0.1 * nrm(ks[9], (DEPTH, 2, RET_HEADS), F32)
    na_rpb = 0.05 * nrm(ks[10], (DEPTH, NA_HEADS, 2 * WIN_H - 1, 2 * WIN_W - 1), F32)
    w_out = nrm(ks[11], (DEPTH, MIX_W, D_MODEL), F32) * (DEEPNORM_BETA * MIX_W ** -0.5)
    ln_g = 1.0 + 0.01 * nrm(ks[12], (DEPTH, D_MODEL), F32)
    ln_b = 0.01 * nrm(ks[13], (DEPTH, D_MODEL), F32)
    return {'x': x, 'c': c, 'ctx': ctx, 'c_ctx': c_ctx, 'w_mod': w_mod, 'b_mod': b_mod,
            'w_in': w_in, 'conv_w': conv_w, 'conv_b': conv_b, 'ret_decay': ret_decay,
            'na_rpb': na_rpb, 'w_out': w_out, 'ln_g': ln_g, 'ln_b': ln_b}

def second_block(x, c, ctx, c_ctx, w_mod, b_mod, w_in, conv_w, conv_b, ret_decay, na_rpb,
              w_out, ln_g, ln_b):
    c_act = jax.nn.silu(c)
    cc_act = jax.nn.silu(c_ctx)
    xc = ctx
    for l in range(DEPTH):
        x, xc = hybrid_layer(x, xc, c_act, cc_act, w_mod[l], b_mod[l], w_in[l], conv_w[l], conv_b[l],
                             ret_decay[l], na_rpb[l], w_out[l], ln_g[l], ln_b[l],
                             need_ctx=(l < DEPTH - 1))
    return x


def setup_inputs(seed=0):
    out = dict(first_inputs(seed))
    for name, value in second_inputs(seed + 1).items():
        if name != "x":
            out[name + "_2"] = value
    return out


def reference(
    x, rel_bias, attn_pre_norm, attn_w_in, attn_w_out, attn_post_norm, ssm_pre_norm, ssm_w_in,
    ssm_a_re, ssm_a_im, ssm_log_dt, ssm_b_re, ssm_b_im, ssm_c_re, ssm_c_im, ssm_d, ssm_w_glu,
    ssm_b_glu, ssm_w_out, ssm_post_norm, c_2, ctx_2, c_ctx_2, w_mod_2, b_mod_2, w_in_2,
    conv_w_2, conv_b_2, ret_decay_2, na_rpb_2, w_out_2, ln_g_2, ln_b_2,
):
    x = first_block(
        x, rel_bias, attn_pre_norm, attn_w_in, attn_w_out, attn_post_norm, ssm_pre_norm,
        ssm_w_in, ssm_a_re, ssm_a_im, ssm_log_dt, ssm_b_re, ssm_b_im, ssm_c_re, ssm_c_im, ssm_d,
        ssm_w_glu, ssm_b_glu, ssm_w_out, ssm_post_norm,
    )
    return second_block(
        x, c_2, ctx_2, c_ctx_2, w_mod_2, b_mod_2, w_in_2, conv_w_2, conv_b_2, ret_decay_2,
        na_rpb_2, w_out_2, ln_g_2, ln_b_2,
    )


_drawn_inputs = setup_inputs


def setup_inputs(seed=0):
    import zlib

    import numpy as np

    out = dict(_drawn_inputs(seed))
    spreads = {}
    factors = {'ssm_a_re': 8.0,
     'ssm_b_glu': 8.0,
     'ctx_2': 5.216,
     'c_ctx_2': 3.631,
     'b_mod_2': 5.973,
     'conv_b_2': 8.0,
     'na_rpb_2': 8.0,
     'ln_g_2': 3.816,
     'ln_b_2': 3.932}
    for name, (base, spread) in spreads.items():
        noise = np.random.default_rng([zlib.crc32(name.encode()), seed]).standard_normal(out[name].shape)
        drawn = base * np.exp(spread * noise) if base else spread * noise
        out[name] = __import__('jax').numpy.asarray(drawn.astype(out[name].dtype))
    for name, factor in factors.items():
        out[name] = (out[name] * factor).astype(out[name].dtype)
    return out
```

```python
from contextlib import ExitStack
import math

import numpy as np
import concourse.bass as bass
from concourse import mybir

F32 = mybir.dt.float32
F32R = mybir.dt.float32r
ALU = mybir.AluOpType
ACT = mybir.ActivationFunctionType
AX = mybir.AxisListType
NEG = -1e30

P = 128
D = 1024
KT = D // P
S = 1024
NT = S // P
CTX = 256
HP = 8
GROUPS = ((128, 1), (512, 4), (2048, 16))
RMS_EPS = 1e-6
LN_EPS = 1e-5
SCALE = 0.125


def t5_bucket(dist):
    n = np.maximum(dist, 1).astype(np.float32)
    large = 16 + (np.log(n / np.float32(16)) / np.float32(math.log(2048 / 16)) * np.float32(16)).astype(np.int32)
    return np.where(dist < 16, dist, np.minimum(large, 31))


def bias_onehot():
    hot = np.zeros((33, 3, 384), np.float32)
    for g, (_, dil) in enumerate(GROUPS):
        for k in range(384):
            back = (255 if g < 2 else 127) - k
            if 0 <= back <= 128:
                hot[int(t5_bucket(np.array([back * dil]))[0]), g, k] = 1.0
            else:
                hot[32, g, k] = 1.0
    return hot.reshape(33, 3 * 384)


I32 = mybir.dt.int32
MAGIC = 12582912.0
K_LOADS = 16
Q_OPS = 4 + 4 * (15 + 7 + 7)


def parts_of(x, bits):
    out = []
    for _ in range(3):
        e = math.floor(math.log2(abs(x))) if x else 0
        q = 2.0 ** (e - bits + 1)
        out.append(math.floor(x / q) * q)
        x -= out[-1]
    return out


LN2_HI = parts_of(math.log(2.0), 14)[0]
LN2_LO = math.log(2.0) - LN2_HI
TWO_PI_1, TWO_PI_2, TWO_PI_3 = parts_of(2 * math.pi, 9)[0], parts_of(2 * math.pi, 9)[1], None
TWO_PI_3 = 2 * math.pi - TWO_PI_1 - TWO_PI_2
PI_BELOW = float(np.nextafter(np.float32(math.pi), np.float32(0)))

def retention_constants():
    i = np.arange(P, dtype=np.float32)
    col = i[:, None]
    perm = np.zeros((P, P), np.float32)
    perm[np.arange(P) ^ 16, np.arange(P)] = 1.0
    ones = (np.arange(P)[:, None] // 64 == np.arange(P)[None] // 64).astype(np.float32) / 64
    full = np.ones((P, 1), np.float32)
    return np.concatenate([np.maximum(i[None] - col, 0), np.maximum(col - i[None], 0), full * (i + 1)[None],
                           full * (P - i)[None], P - 1 - col, col, ones, perm], 1).astype(np.float32)


def rope_tables():
    t = np.arange(S)
    inv = (np.float32(10000.0) ** (-np.arange(16, dtype=np.float32) / np.float32(16))).astype(np.float32)
    row = (t // 64).astype(np.float32)[:, None] * inv
    col = (t % 64).astype(np.float32)[:, None] * inv
    cos = [np.cos(a) for a in (row, row, col, col)] * 2
    sin = [s * np.sin(a) for s, a in ((-1, row), (1, row), (-1, col), (1, col))] * 2
    return np.stack([np.concatenate(cos, 1).T, np.concatenate(sin, 1).T]).astype(np.float32)


def window_mask():
    q = np.arange(64)
    first = np.clip(q - 8, 0, 48)
    inside = (q[None] >= first[:, None]) & (q[None] < first[:, None] + 16)
    return np.tile(np.where(inside, np.float32(0), np.float32(NEG)), (2, 1)).astype(np.float32)


def constants():
    return {"c_onehot": bias_onehot(), "c_ident": np.eye(P, dtype=np.float32), "c_ret": retention_constants(),
            "c_rope": rope_tables(), "c_nmask": window_mask()}


L1_PER_HP = 10
N_L1 = HP * L1_PER_HP
SLOT_F1 = N_L1
SLOT_U = SLOT_F1 + 2 * KT
SLOT_L3 = (SLOT_U + 4 * 2 * KT, SLOT_U + 4 * 2 * KT + 32 + 3 * KT)
N_SLOTS = SLOT_L3[1] + 32 + 2 * KT

STAGES_DONE = 12
T_DONE, F_DONE, Y_DONE = 2 * NT, 2 * NT, KT
CONST_DONE, FC_DONE = 4, 2
U_DONE, VT_DONE = 3 * NT * HP, 6 * HP


def build(nc, io, out):
    x_in = io["x"].rearrange("b s d -> (b s) d")
    ctx = ExitStack()
    with ctx:
        def sb(name, shape, dt=F32):
            return ctx.enter_context(nc.sbuf_tensor(name, shape, dt))

        def sem(name):
            return ctx.enter_context(nc.semaphore(name))

        def dram(name, shape):
            return nc.dram_tensor(name, shape, F32, kind="Internal").ap()

        act_hi = sb("act_hi", [P, KT, S + CTX], F32R)
        act_lo = sb("act_lo", [P, KT, S + CTX], F32R)
        w_raw = sb("w_raw", [P, 2, 1024])
        w_hi = sb("w_hi", [P, 2, 1024], F32R)
        w_lo = sb("w_lo", [P, 2, 1024], F32R)
        ident = sb("ident", [P, P])
        one = sb("one", [P, 1])
        arena = sb("arena", [P, 26300])
        psum = ctx.enter_context(nc.psum_tensor("psum", [P, 8, 512], F32))

        def region(at, *shape):
            n = int(np.prod(shape))
            assert at + n <= 26300, (at, shape)
            v = arena[:, at:at + n]
            if len(shape) == 2:
                v = v.rearrange("p (a b) -> p a b", a=shape[0])
            if len(shape) == 3:
                v = v.rearrange("p (a b c) -> p a b c", a=shape[0], b=shape[1])
            return v

        slot_loaded = [sem("slot_loaded0"), sem("slot_loaded1")]
        one_set = sem("one_set")
        slot_hi = sem("slot_hi")
        slot_split = sem("slot_split")
        slot_used = sem("slot_used")
        stage_done = sem("stage_done")

        stages = [0]

        def stage_end(eng, n):
            eng.drain().then_inc(stage_done, 1)
            eng.wait_ge(stage_done, 3 * n)

        t_loaded = [sem("t_loaded0"), sem("t_loaded1")]
        t_square, t_var, t_root, t_rstd, t_scaled, t_turned, t_full_act, t_full_dve, t_hi, t_lo = [
            sem(n) for n in ("t_square", "t_var", "t_root", "t_rstd", "t_scaled", "t_turned",
                             "t_full_act", "t_full_dve", "t_hi", "t_lo")]
        T_ROWS = region(8192, 2, 1024)
        T_NORM = region(8192 + 2048, 2, 1024)
        T_FULL = region(8192 + 4096, 2, 1024)
        T_STAT = region(8192 + 6144, 2, 4)
        T_GAIN = region(8192 + 6152, 2, 8)
        T_ROOM = 8192

        def t_src_rows(src, order8):
            if order8:
                return lambda t: src.rearrange("(p s) d -> s p d", s=8)[t]
            return lambda t: src[bass.ds(t * P, P), :]

        def t_act(act, base, tiles, rows, norm, gain, dst0):
            if rows is not None:
                for b in range(2):
                    act.dma_start(T_ROWS[:, b], rows(b)).then_inc(t_loaded[b], 16)
            for t in range(tiles):
                b, n = t % 2, base + t
                if norm:
                    act.wait_ge(t_loaded[b], 16 * (base // 2 + t // 2 + 1))
                    if n >= 2:
                        act.wait_ge(t_turned, n - 1)
                    nc.scalar.activation(T_NORM[:, b], T_ROWS[:, b], ACT.Square,
                                         accum_out=T_STAT[:, b, 0:1]).then_inc(t_square, 1)
                    act.wait_ge(t_var, n + 1)
                    nc.scalar.activation(T_STAT[:, b, 2:3], T_STAT[:, b, 1:2], ACT.Sqrt).then_inc(t_root, 1)
                act.wait_ge(t_turned, n + 1)
                if n >= 2:
                    act.wait_ge(t_lo, n - 1)
                for k in range(4):
                    ins = nc.scalar.activation(T_FULL[:, b, k * P:(k + 1) * P], T_PS(b)[:, k * P:(k + 1) * P],
                                               ACT.Identity, scale=gain[:, 0, k:k + 1],
                                               bias=gain[:, 1, k:k + 1])
                ins.then_inc(t_full_act, 1)
                act.wait_ge(t_full_act, n + 1)
                act.wait_ge(t_full_dve, n + 1)
                nc.scalar.copy(act_hi[:, :, dst0 + t * P:dst0 + (t + 1) * P],
                               T_FULL[:, b].rearrange("p (k c) -> p k c", k=KT)).then_inc(t_hi, 1)
                if rows is not None and t + 2 < tiles:
                    act.wait_ge(t_scaled, n + 1)
                    act.dma_start(T_ROWS[:, b], rows(t + 2)).then_inc(t_loaded[b], 16)

        def t_dve(dve, base, tiles, norm, gain, dst0):
            for t in range(tiles):
                b, n = t % 2, base + t
                if norm:
                    dve.wait_ge(t_square, n + 1)
                    nc.vector.tensor_scalar(T_STAT[:, b, 1:2], T_STAT[:, b, 0:1], 1.0 / D, RMS_EPS,
                                            ALU.mult, ALU.add).then_inc(t_var, 1)
                    dve.wait_ge(t_root, n + 1)
                    nc.vector.reciprocal(T_STAT[:, b, 3:4], T_STAT[:, b, 2:3]).then_inc(t_rstd, 1)
                    dve.wait_ge(t_rstd, n + 1)
                    nc.vector.tensor_scalar(T_NORM[:, b], T_ROWS[:, b], T_STAT[:, b, 3:4], None,
                                            ALU.mult).then_inc(t_scaled, 1)
                else:
                    dve.wait_ge(t_loaded[b], 16 * (base // 2 + t // 2 + 1))
                    if n >= 2:
                        dve.wait_ge(t_turned, n - 1)
                    nc.vector.tensor_copy(T_NORM[:, b], T_ROWS[:, b]).then_inc(t_scaled, 1)
                dve.wait_ge(t_turned, n + 1)
                if n >= 2:
                    dve.wait_ge(t_hi, n - 1)
                for k in range(4, 8):
                    ins = nc.vector.tensor_scalar(T_FULL[:, b, k * P:(k + 1) * P], T_PS(b)[:, k * P:(k + 1) * P],
                                                  gain[:, 0, k:k + 1], gain[:, 1, k:k + 1],
                                                  ALU.mult, ALU.add)
                ins.then_inc(t_full_dve, 1)
                dve.wait_ge(t_hi, n + 1)
                cols = slice(dst0 + t * P, dst0 + (t + 1) * P)
                nc.vector.tensor_tensor(act_lo[:, :, cols], T_FULL[:, b].rearrange("p (k c) -> p k c", k=KT),
                                        act_hi[:, :, cols].bitcast(F32), ALU.subtract).then_inc(t_lo, 1)

        def T_PS(b):
            return psum[:, 2 * b:2 * b + 2, :].rearrange("p a c -> p (a c)")

        def t_pe(pe, base, tiles):
            for t in range(tiles):
                b, n = t % 2, base + t
                pe.wait_ge(t_scaled, n + 1)
                if n >= 2:
                    pe.wait_ge(t_full_act, n - 1)
                    pe.wait_ge(t_full_dve, n - 1)
                for k in range(KT):
                    ins = nc.tensor.transpose(T_PS(b)[:, k * P:(k + 1) * P], T_NORM[:, b, k * P:(k + 1) * P],
                                              ident[:, :])
                ins.then_inc(t_turned, 1)

        PASSES = ((w_hi, act_hi), (w_hi, act_lo), (w_lo, act_hi))

        def mul_t(pe, n, par, banks, segs):
            pe.wait_ge(slot_split, n + 3)
            for k in range(KT):
                for w, a in PASSES:
                    for bank, (c0, c) in zip(banks, segs):
                        ins = nc.tensor.matmul(psum[:, bank, 0:c], w[:, par, k * P:(k + 1) * P],
                                               a[:, k, c0:c0 + c], start=(k == 0 and a is act_hi and w is w_hi),
                                               stop=(k == KT - 1 and w is w_lo))
            ins.then_inc(slot_used, 1)

        def mul_r(pe, n, par, k, tiles):
            pe.wait_ge(slot_split, n + 3)
            for j, t in enumerate(tiles):
                for w, a in PASSES:
                    for c in range(2):
                        ins = nc.tensor.matmul(psum[:, 2 * j + c, :], a[:, k, t * P:(t + 1) * P],
                                               w[:, par, c * 512:(c + 1) * 512],
                                               start=(k == 0 and a is act_hi and w is w_hi),
                                               stop=(k == KT - 1 and w is w_lo))
            ins.then_inc(slot_used, 1)

        y_hi, y_lo = sem("y_hi"), sem("y_lo")

        def by8(v):
            return v.rearrange("p (q s) -> p s q", s=8)

        def by_block(v):
            return v.rearrange("p (s q) -> p s q", q=P)

        def y_act(act, base, src, order8, cols=S):
            for k in range(KT):
                v = by8(src[:, k]) if order8 else by_block(src[:, k, 0:cols])
                nc.scalar.copy(by_block(act_hi[:, k, 0:cols]), v).then_inc(y_hi, 1)

        def y_dve(dve, base, src, order8, cols=S):
            for k in range(KT):
                dve.wait_ge(y_hi, base + k + 1)
                v = by8(src[:, k]) if order8 else by_block(src[:, k, 0:cols])
                nc.vector.tensor_tensor(by_block(act_lo[:, k, 0:cols]), v,
                                        by_block(act_hi[:, k, 0:cols]).bitcast(F32), ALU.subtract).then_inc(y_lo, 1)

        f_loaded = [sem("f_loaded0"), sem("f_loaded1")]
        f_stored = [sem("f_stored0"), sem("f_stored1")]
        f_const = sem("f_const")
        r_mul, f_square, f_var, f_root, f_rstd, f_scaled, f_sum = [
            sem(n) for n in ("r_mul", "f_square", "f_var", "f_root", "f_rstd", "f_scaled", "f_sum")]
        F_GAIN = region(0, 1024)
        F_X = region(1024, 2, 1024)
        F_T = region(3072, 2, 1024)
        F_ST = region(5120, 2, 4)

        def ps_tile(j):
            return psum[:, 2 * j:2 * j + 2, :].rearrange("p a c -> p (a c)")

        def spread_rows(v):
            n = v.shape[-1]
            return bass.AP(tensor=v.tensor, offset=v.offset, ap=[[0, P], [1, n]])

        def r_pe(pe, slot0, passes, free, base):
            done = 0
            for p, tiles in enumerate(passes):
                for k in range(KT):
                    if k == 0 and p > 0:
                        pe.wait_ge(free, base + done)
                    mul_r(pe, slot0 + KT * p + k, k % 2, k, tiles)
                done += len(tiles)

        def f_act(act, base, slot0, passes, xrows, orows, gain):
            tiles = [t for p in passes for t in p]
            act.dma_start(F_GAIN, spread_rows(gain)).then_inc(f_const, 16)
            for n in range(2):
                act.dma_start(F_X[:, n], xrows(tiles[n])).then_inc(f_loaded[n], 16)
            n = 0
            for p, ts in enumerate(passes):
                act.wait_ge(slot_used, slot0 + KT * (p + 1) + 2)
                for j, t in enumerate(ts):
                    b, m = n % 2, base + n
                    if n >= 2:
                        act.wait_ge(f_stored[b], 16 * (m // 2))
                    nc.scalar.activation(F_T[:, b], ps_tile(j), ACT.Square, accum_out=F_ST[:, b, 0:1]).then_inc(f_square, 1)
                    act.wait_ge(f_var, m + 1)
                    nc.scalar.activation(F_ST[:, b, 2:3], F_ST[:, b, 1:2], ACT.Sqrt).then_inc(f_root, 1)
                    act.wait_ge(f_sum, m + 1)
                    act.dma_start(orows(t), F_T[:, b]).then_inc(f_stored[b], 16)
                    if n + 2 < len(tiles):
                        act.dma_start(F_X[:, b], xrows(tiles[n + 2])).then_inc(f_loaded[b], 16)
                    n += 1
            for b in range(2):
                act.wait_ge(f_stored[b], 16 * ((base + n) // 2))

        def f_dve(dve, base, passes, const_n):
            n = 0
            dve.wait_ge(f_const, 16 * const_n)
            for ts in passes:
                for j, t in enumerate(ts):
                    b, m = n % 2, base + n
                    dve.wait_ge(f_square, m + 1)
                    nc.vector.tensor_scalar(F_ST[:, b, 1:2], F_ST[:, b, 0:1], 1.0 / D, RMS_EPS,
                                            ALU.mult, ALU.add).then_inc(f_var, 1)
                    dve.wait_ge(f_root, m + 1)
                    nc.vector.reciprocal(F_ST[:, b, 3:4], F_ST[:, b, 2:3]).then_inc(f_rstd, 1)
                    dve.wait_ge(f_rstd, m + 1)
                    nc.vector.scalar_tensor_tensor(F_T[:, b], ps_tile(j), F_ST[:, b, 3:4], F_GAIN,
                                                   ALU.mult, ALU.mult).then_inc(f_scaled, 1)
                    dve.wait_ge(f_scaled, m + 1)
                    dve.wait_ge(f_loaded[b], 16 * (m // 2 + 1))
                    nc.vector.tensor_tensor(F_T[:, b], F_T[:, b], F_X[:, b], ALU.add).then_inc(f_sum, 1)
                    n += 1

        HALVES = ((0, 1, 2, 3), (4, 5, 6, 7))

        def rows8(v):
            return lambda t: v.rearrange("(q s) d -> s q d", s=8)[t]

        def rows(v):
            return lambda t: v[t * P:(t + 1) * P, :]

        x_turned, x_hi, x_lo = sem("x_turned"), sem("x_hi"), sem("x_lo")

        def x_pe(pe, base, src, tiles):
            for t in range(tiles):
                j = t % 4
                if t >= 4:
                    pe.wait_ge(x_lo, base + t - 3)
                for k in range(KT):
                    ins = nc.tensor.transpose(ps_tile(j)[:, k * P:(k + 1) * P], src[:, t, k * P:(k + 1) * P], ident[:, :])
                ins.then_inc(x_turned, 1)

        def x_dst(a, t, order8):
            if order8:
                return a[:, :, 0:S].rearrange("p k (q s) -> p s k q", s=8)[:, t]
            return a[:, :, t * P:(t + 1) * P]

        def x_act(act, base, tiles, order8):
            for t in range(tiles):
                act.wait_ge(x_turned, base + t + 1)
                nc.scalar.copy(x_dst(act_hi, t, order8),
                               ps_tile(t % 4).rearrange("p (k c) -> p k c", k=KT)).then_inc(x_hi, 1)

        def x_dve(dve, base, tiles, order8):
            for t in range(tiles):
                dve.wait_ge(x_hi, base + t + 1)
                nc.vector.tensor_tensor(x_dst(act_lo, t, order8), ps_tile(t % 4).rearrange("p (k c) -> p k c", k=KT),
                                        x_dst(act_hi, t, order8).bitcast(F32), ALU.subtract).then_inc(x_lo, 1)

        x1 = dram("x1", (S, D))
        x2 = dram("x2", (S, D))

        F_T2 = region(8192, 2, 1024)
        k_part, s_zero = sem("k_part"), sem("s_zero")
        G2 = 32
        U = region(0, 64, P)
        ST = region(8192, G2, 2, 129)
        YR = region(16448, 8, 1024)
        SP_RING = region(24640, 2, 512)
        UT = region(25664, 2, 256)
        b_mat = dram("b_mat", (G2, P, 256))
        c_mat = dram("c_mat", (G2, P, 256))
        k_mat = dram("k_mat", (16, 64, 256))
        m_mat = dram("m_mat", (G2, P, 256))
        z_rows = dram("z_rows", (S, D))
        q_pow = dram("q_pow", (P, 1024))
        k_load, k_chain, k_turned, k_c, k_arg, k_trig = [sem(n) for n in (
            "k_load", "k_chain", "k_turned", "k_c", "k_arg", "k_trig")]
        k_b, k_bt, k_bcopy, k_cp, k_conv, k_kk, k_stored = [sem(n) for n in (
            "k_b", "k_bt", "k_bcopy", "k_cp", "k_conv", "k_kk", "k_stored")]
        k_bst = [sem("k_bst0"), sem("k_bst1")]
        k_kst = [sem("k_kst0"), sem("k_kst1")]
        z_tanh, z_scaled = sem("z_tanh"), sem("z_scaled")
        z_stored = [sem("z_stored0"), sem("z_stored1")]
        u_copied = sem("u_copied")
        s_loaded = [sem("s_loaded0"), sem("s_loaded1")]
        s_turned, s_ut, s_mul, s_out = sem("s_turned"), sem("s_ut"), sem("s_mul"), sem("s_out")
        q_loaded, q_dve = sem("q_loaded"), sem("q_dve")
        h_const, h_sum, h_gate, h_part, h_done, e_gelu = [sem(n) for n in ("h_const", "h_sum", "h_gate", "h_part", "h_done", "e_gelu")]
        h_z = [sem("h_z0"), sem("h_z1")]

        places = [0]

        def take(*shape):
            at = places[0]
            places[0] += int(np.prod(shape))
            return region(at, *shape)

        KA = take(24, 32)
        KP = take(2, 9, 32)
        KQ = take(2, 16, 32)
        KB = take(2, 32, 16)
        KBB = take(2, 32, 16)
        KC = take(2, 32, 16)
        KBP = take(32, 8, 16)
        KCP = take(2, 32, 144)
        KCL = take(2, 8, 128)
        KT1 = take(32, 16)
        KBT = take(2, 512)
        KK = take(2, 2, 512)
        KD = take(64, 16)
        KZ = KT1[0:16].rearrange("p a b -> p (a b)")
        QRR = region(16448, 32, 2, 16)
        QIS = region(17472, 32, 2, 16)
        Q1 = region(18496, 32, 2, 16)
        Q2 = region(19520, 32, 2, 16)

        Y1 = region(0, KT, 1024)
        QKV = region(8192, 9, 1024)
        GATE = region(17408, 1024)
        VROW = region(18432, 8, P)
        LOG = region(19456, 2, 512)
        PT = region(20480, 2, 512)
        BIAS = region(21504, 2, 640)
        STAT = region(22784, 2, 8)
        WIDE = region(22800, 2, 256)
        bias_rows = dram("bias_rows", (16, 1152))
        bias_mat = dram("bias_mat", (16, P, 512))
        bias_mat2 = dram("bias_mat2", (16, 64, 64))

        const_loaded = sem("const_loaded")
        b_spread, b_copied, b_stored, b_skewed = sem("b_spread"), sem("b_copied"), sem("b_stored"), sem("b_skewed")
        a_bias, a_neg = sem("a_bias"), sem("a_neg")
        g_evac = [sem("g_evac0"), sem("g_evac1")]
        g_gate = sem("g_gate")
        u_scores, u_logits, u_negmax, u_probs, u_turned, u_pt, u_out, u_wide, u_evac = [
            sem(n) for n in ("u_scores", "u_logits", "u_negmax", "u_probs", "u_turned", "u_pt", "u_out", "u_wide",
                             "u_evac")]
        v_turned, v_rows = sem("v_turned"), [sem("v_rows_act"), sem("v_rows_dve")]
        c_dve, c_diff, c_act = sem("c_dve"), sem("c_diff"), sem("c_act")
        c_zero = sem("c_zero")
        c_free = sem("c_free")
        UNITS = [(g, u) for g in range(3) for u in range(NT)]
        NU = len(UNITS)
        MERGE = (0, 2, 1)

        def OB(n):
            return 4 + 3 * (n % 2)

        def key_tiles(g, u):
            if g == 2 or (g == 0 and u == 0) or (g == 1 and u % 2 == 0):
                return [u]
            return [u - 1, u]

        def bias_cols(g, u):
            n = len(key_tiles(g, u))
            return slice(512, 640) if g == 2 else slice(256 * g + 256 - 128 * n, 256 * g + 256)

        def scatter(view, g):
            d = GROUPS[g][1]
            return view.rearrange("p (r m) -> p m r", r=d) if d > 1 else view

        SLOT_OF = [6, 7, 8, 3, 4, 5, 0, 1, "gate", 2]

        def slot_col(j, hp):
            p = SLOT_OF[j]
            if p == "gate":
                return 9 * D + hp * P
            return (p % 3) * 3 * D + (p // 3) * D + hp * P

        def evac_qkv(j):
            p = SLOT_OF[j]
            g, d = p // 3, GROUPS[p // 3][1]
            for half in range(2):
                src = psum[:, 2 * (j % 2) + half, :]
                dst = QKV[:, p]
                if d > 1:
                    src = src.rearrange("p (m r) -> p m r", r=d)
                    dst = dst.rearrange("p (r m) -> p m r", r=d)[:, half * (512 // d):(half + 1) * (512 // d), :]
                else:
                    dst = dst[:, half * 512:(half + 1) * 512]
                ins = nc.scalar.activation(dst, src, ACT.Copy, scale=SCALE if p % 3 == 0 else 1.0)
            return ins

        onehot = region(0, 1152)
        relb = region(1152, 16)
        spread = region(1200, 3, 384)

        c_cols = sb("c_cols", [P, KT, 2])
        W_MOD = region(8192, 2, 3072)
        M_ROW = region(14400, 3072)
        M_BIAS = region(17472, 3072)
        mod_rows = dram("mod_rows", (2, 2, 3072))
        m_c, m_silu, m_mul, m_sum, m_stored = sem("m_c"), sem("m_silu"), sem("m_mul"), sem("m_sum"), sem("m_stored")
        m_bias = sem("m_bias")
        m_w = [sem("m_w0"), sem("m_w1")]

        def m_pe(pe, l):
            pe.wait_ge(m_silu, 1)
            for k in range(KT):
                n = KT * l + k
                pe.wait_ge(m_w[k % 2], 16 * (n // 2 + 1))
                for c in range(6):
                    ins = nc.tensor.matmul(psum[0:2, c, :], c_cols[:, k, :], W_MOD[:, k % 2, c * 512:(c + 1) * 512],
                                           start=(k == 0), stop=(k == KT - 1))
                ins.then_inc(m_mul, 1)

        def m_act(act, l):
            w = io["w_mod_2"][l]
            for k in range(2):
                act.dma_start(W_MOD[:, k], w[k * P:(k + 1) * P, :]).then_inc(m_w[k % 2], 16)
            act.dma_start(M_BIAS[0:2, :], bass.AP(tensor=io["b_mod_2"].tensor, offset=io["b_mod_2"].offset + 3072 * l,
                                                  ap=[[0, 2], [1, 3072]])).then_inc(m_bias, 16)
            if l == 0:
                act.wait_ge(m_c, 32)
                nc.scalar.activation(c_cols[:, :, :], c_cols[:, :, :], ACT.Silu).then_inc(m_silu, 1)
            for k in range(2, KT):
                act.wait_ge(m_mul, KT * l + k - 1)
                act.dma_start(W_MOD[:, k % 2], w[k * P:(k + 1) * P, :]).then_inc(m_w[k % 2], 16)
            act.wait_ge(m_sum, l + 1)
            act.dma_start(mod_rows[l], M_ROW[0:2, :]).then_inc(m_stored, 16)
            act.wait_ge(m_stored, 16 * (l + 1))

        def m_dve(dve, l):
            dve.wait_ge(m_mul, KT * (l + 1))
            dve.wait_ge(m_bias, 16 * (l + 1))
            nc.vector.tensor_tensor(M_ROW[0:2, :], psum[0:2, 0:6, :].rearrange("p a c -> p (a c)"), M_BIAS[0:2, :],
                                    ALU.add).then_inc(m_sum, 1)

        TT = S + CTX
        NC = TT // P
        Y2 = region(0, KT, TT)
        TK, TV, TQ, TG = (region(10240 + i * TT, TT) for i in range(4))
        KF, KBW, VR = (region(15360 + i * TT, NC, P) for i in range(3))
        SFB = region(19200, 2, NC, P)
        ROPE = region(19200, 2, S)
        RO = region(21760, TT)
        TMP = region(23040, TT)
        CON = region(24320, 770)
        C_A, C_B, C_UP, C_DOWN = (CON[:, i * P:(i + 1) * P] for i in range(4))
        C_COLS = CON[:, 512:514]
        C_ONES, C_PERM = CON[:, 514:642], CON[:, 642:770]
        DM = region(25090, 2, P)
        WQ = region(25346, 2, P)
        SD = region(25602, 2, 256)
        LG = region(26114, 12)
        LGP = region(26126, 2)
        GC = region(26128, 2)
        WK = region(26130, 4)
        LT = region(26140, 4, 12)
        x3 = dram("x3", (S, D))
        xc3 = dram("xc3", (CTX, D))
        p_evac = sem("p_evac")
        p_const = sem("p_const")
        r_lgc, r_l1, r_l2 = sem("r_lgc"), sem("r_l1"), sem("r_l2")
        r_lg, r_exp, r_rope, r_swap, r_vt, r_kt, r_rows, r_u, r_chain, r_scan = [sem(n) for n in (
            "r_lg", "r_exp", "r_rope", "r_swap", "r_vt", "r_kt", "r_rows", "r_u", "r_chain", "r_scan")]
        r_s, r_sd, r_omul, r_o, r_mean, r_cent, r_sq, r_var, r_eps, r_root, r_table, r_done = [sem(n) for n in (
            "r_s", "r_sd", "r_omul", "r_o", "r_mean", "r_cent", "r_sq", "r_var", "r_eps", "r_root", "r_table", "r_done")]
        SEGS = ((0, 512), (512, 512), (1024, 256))
        HALF = (slice(0, 64), slice(64, 128))

        def flat(b0, n):
            return psum[:, b0:b0 + n, :].rearrange("p a c -> p (a c)")

        def segs_of(l, key):
            return SEGS if l == 0 or key else SEGS[:2]

        def p_slot(pe, l, m, par, key):
            pe.wait_ge(p_evac, m + 1)
            mul_t(pe, SLOT_L3[l] + m - 32 * l, par, tuple(range(3 * par, 3 * par + len(segs_of(l, key)))), segs_of(l, key))

        def p_take(act, l, m, par, key, dst, func=ACT.Copy, scale=1.0):
            n = TT if len(segs_of(l, key)) == 3 else S
            act.wait_ge(slot_used, SLOT_L3[l] + m - 32 * l + 3)
            nc.scalar.activation(dst[:, 0:n], flat(3 * par, 3)[:, 0:n], func, scale=scale).then_inc(p_evac, 1)

        def chunks(l):
            return NC if l == 0 else NT

        FWD = (8, 9, 0, 1, 2, 3, 4, 5, 6, 7)
        BWD = (9, 8, 7, 6, 5, 4, 3, 2, 1, 0)

        def ret_pe(pe, l):
            with pe.Fori(0, 3) as hp:
                it = hp + 3 * l
                m = 4 * hp + 32 * l
                for j in range(4):
                    p_slot(pe, l, m + j, j % 2, j < 2)
                pe.wait_ge(p_evac, m + 4 + 2)
                for i, t in enumerate((TK, TQ)):
                    for c in range(2):
                        ins = nc.tensor.matmul(psum[:, 2 * i + c, :], C_PERM, t[:, c * 512:(c + 1) * 512], start=True, stop=True)
                    ins.then_inc(r_swap, 1)
                for n in range(NC):
                    ins = nc.tensor.transpose(psum[:, 4 + n // 4, (n % 4) * P:(n % 4 + 1) * P], TV[:, n * P:(n + 1) * P], ident[:, :])
                ins.then_inc(r_vt, 1)
                pe.wait_ge(r_rope, 2 * it + 2)
                for n in range(NC):
                    ins = nc.tensor.transpose(psum[:, n // 4, (n % 4) * P:(n % 4 + 1) * P], TK[:, n * P:(n + 1) * P], ident[:, :])
                ins.then_inc(r_kt, 1)
                pe.wait_ge(r_rows, it + 1)
                for i, w in enumerate((KF, KBW)):
                    for n in range(NC):
                        ins = nc.tensor.matmul(psum[:, UBANK[i][n // 4], (n % 4) * P:(n % 4 + 1) * P], w[:, n], VR[:, n],
                                               start=True, stop=True)
                ins.then_inc(r_u, 1)
                pe.wait_ge(r_scan, it + 1)

                def inner(n):
                    if n >= 2:
                        pe.wait_ge(r_sd, chunks(l) * hp + (n - 1) + RC0[l])
                    for h in range(2):
                        ins = nc.tensor.matmul(psum[:, 2 * (n % 2) + h, 0:P], TK[HALF[h], n * P:(n + 1) * P],
                                               TQ[HALF[h], n * P:(n + 1) * P], start=True, stop=True)
                    ins.then_inc(r_s, 1)

                def out_of(n):
                    if n >= 2:
                        pe.wait_ge(r_o, chunks(l) * hp + (n - 1) + RC0[l])
                    o = psum[:, 4 + n % 2, 0:P]
                    nc.tensor.matmul(o, SFB[:, 0, n], TV[:, n * P:(n + 1) * P], start=True, stop=False, skip_group_check=True)
                    nc.tensor.matmul(o, SFB[:, 1, n], TMP[:, n * P:(n + 1) * P], start=False, stop=False, skip_group_check=True)
                    pe.wait_ge(r_sd, chunks(l) * hp + (n + 1) + RC0[l])
                    for h in range(2):
                        ins = nc.tensor.matmul(psum[HALF[h], 4 + n % 2, 0:P], VR[:, n, 64 * h:64 * h + 64],
                                               SD[:, n % 2, h * P:(h + 1) * P], start=False, stop=True, skip_group_check=True)
                    ins.then_inc(r_omul, 1)

                inner(0)
                for n in range(chunks(l)):
                    if n + 1 < chunks(l):
                        inner(n + 1)
                    out_of(n)
                pe.wait_ge(r_o, chunks(l) * hp + chunks(l) + RC0[l])
                for i, (c0, c) in enumerate(segs_of(l, False)):
                    ins = nc.tensor.matmul(psum[:, 5 + i, 0:c], C_ONES, RO[:, c0:c0 + c], start=True, stop=True)
                ins.then_inc(r_mean, 1)
                pe.wait_ge(r_sq, it + 1)
                for i, (c0, c) in enumerate(segs_of(l, False)):
                    ins = nc.tensor.matmul(psum[:, i, 0:c], C_ONES, TMP[:, c0:c0 + c], start=True, stop=True)
                ins.then_inc(r_var, 1)
                pe.wait_ge(r_eps, it + 1)

        UBANK = ((3, 4, 5), (6, 7, 0))
        RC0 = (0, 3 * NC)
        RCH = 22

        def ret_act(act, l):
            act.dma_start(CON[:, :], io["c_ret"]).then_inc(p_const, 16)
            act.dma_start(LG[:, :], spread_rows(io["ret_decay_2"][l].rearrange("d h -> (d h)"))).then_inc(p_const, 16)
            act.wait_ge(r_l1, 2 * l + 1)
            nc.scalar.activation(LT[:, 3], LT[:, 3], ACT.Exp).then_inc(r_l2, 1)
            act.wait_ge(r_l1, 2 * l + 2)
            nc.scalar.activation(LT[:, 0], LT[:, 0], ACT.Ln).then_inc(r_l2, 1)
            with act.Fori(0, 3) as hp:
                it = hp + 3 * l
                m = 4 * hp + 32 * l
                act.wait_ge(r_done, it + 1)
                for i in range(2):
                    act.dma_start(ROPE[:, i], io["c_rope"][i]).then_inc(r_table, 16)
                p_take(act, l, m, 0, True, TK, ACT.Copy, SCALE)
                p_take(act, l, m + 1, 1, True, TV)
                p_take(act, l, m + 2, 0, False, TQ)
                p_take(act, l, m + 3, 1, False, TG, ACT.Silu)
                act.wait_ge(r_lg, it + 1)
                exps = [(DM[:, h], DM[:, h], 1.0) for h in range(2)]
                exps += [(WQ[:, 0], C_UP, LGP[:, 0:1]), (WQ[:, 1], C_DOWN, LGP[:, 1:2]), (GC, LGP, float(P))]
                for out_, in_, sc in exps:
                    nc.scalar.activation(out_, in_, ACT.Exp, scale=sc).then_inc(r_exp, 1)
                for i in range(4):
                    d = i // 2
                    nc.scalar.activation(WK[:, i:i + 1], C_COLS[:, d:d + 1], ACT.Exp,
                                         scale=LT[:, 0, i:i + 1]).then_inc(r_exp, 1)
                for n in range(chunks(l)):
                    act.wait_ge(r_omul, chunks(l) * hp + (n + 1) + RC0[l])
                    nc.scalar.copy(RO[:, n * P:(n + 1) * P], psum[:, 4 + n % 2, 0:P]).then_inc(r_o, 1)
                w = P * chunks(l)
                act.wait_ge(r_cent, it + 1)
                nc.scalar.activation(TMP[:, 0:w], RO[:, 0:w], ACT.Square).then_inc(r_sq, 1)
                act.wait_ge(r_eps, it + 1)
                nc.scalar.activation(TMP[:, 0:w], TMP[:, 0:w], ACT.Sqrt).then_inc(r_root, 1)

        def ret_dve(dve, l):
            V = nc.vector
            dve.wait_ge(p_const, 16 * 2 * (l + 1))
            n_lg = [10 * l]

            def ll(ins):
                n_lg[0] += 1
                ins.then_inc(r_lgc, 1)
                dve.wait_ge(r_lgc, n_lg[0])

            ll(V.tensor_scalar(LT[:, 1], LG, -1.0, None, ALU.mult))
            ll(V.tensor_tensor(LT[:, 1], LT[:, 1], LG, ALU.min))
            V.tensor_copy(LT[:, 3], LT[:, 1]).then_inc(r_l1, 1)
            dve.wait_ge(r_l2, 2 * l + 1)
            ll(V.tensor_scalar(LT[:, 1], LT[:, 3], 1.0, None, ALU.add))
            ll(V.tensor_scalar(LT[:, 2], LT[:, 1], -1.0, 1e-30, ALU.add, ALU.add))
            ll(V.reciprocal(LT[:, 2], LT[:, 2]))
            V.tensor_copy(LT[:, 0], LT[:, 1]).then_inc(r_l1, 1)
            dve.wait_ge(r_l2, 2 * l + 2)
            ll(V.tensor_scalar(LT[:, 0], LT[:, 0], 1e-30, None, ALU.add))
            ll(V.tensor_tensor(LT[:, 0], LT[:, 0], LT[:, 2], ALU.mult))
            ll(V.tensor_tensor(LT[:, 0], LT[:, 0], LT[:, 3], ALU.mult))
            ll(V.tensor_scalar(LG, LG, 0.0, None, ALU.min))
            ll(V.tensor_tensor(LG, LG, LT[:, 0], ALU.subtract))
            if l == 0:
                dve.sem_inc(r_done, 1)
            with dve.Fori(0, 3) as hp:
                it = hp + 3 * l
                m = 4 * hp + 32 * l
                n_r = [0]

                def rl(ins):
                    n_r[0] += 1
                    ins.then_inc(r_chain, 1)
                    dve.wait_ge(r_chain, RCH * it + n_r[0])

                pick = LT[:, 0, 0:4].rearrange("p (d h) -> p d h", d=2)
                rl(V.tensor_copy(pick, LG.rearrange("p (d x h) -> p d x h", d=2, h=2)[:, :, bass.ds(hp, 1), :].rearrange("p d x h -> p d (x h)")))
                for h in range(2):
                    rl(V.tensor_copy(LGP[HALF[h], :], pick[HALF[h], :, h]))
                for h in range(2):
                    rl(V.tensor_scalar(DM[:, h], C_B, LT[:, 0, 2 + h:3 + h], None, ALU.mult))
                    rl(V.scalar_tensor_tensor(DM[:, h], C_A, LT[:, 0, h:h + 1], DM[:, h], ALU.mult, ALU.add))
                V.memset(LT[:, 1, 0:1], 0.0).then_inc(r_lg, 1)
                dve.wait_ge(r_table, 32 * it + 32)
                for i, t in enumerate((TK, TQ)):
                    dve.wait_ge(r_swap, 2 * it + i + 1)
                    rl(V.tensor_tensor(t[:, 0:S], t[:, 0:S], ROPE[:, 0], ALU.mult))
                    rl(V.tensor_tensor(TMP[:, 0:S], flat(2 * i, 2), ROPE[:, 1], ALU.mult))
                    V.tensor_tensor(t[:, 0:S], t[:, 0:S], TMP[:, 0:S], ALU.add).then_inc(r_rope, 1)
                    dve.wait_ge(r_rope, 2 * it + i + 1)
                dve.wait_ge(r_vt, it + 1)
                V.tensor_copy(VR[:, :, :], flat(4, 3)[:, 0:TT].rearrange("p (n c) -> p n c", c=P))
                dve.wait_ge(r_exp, 9 * it + 9)
                dve.wait_ge(r_kt, it + 1)
                kt = flat(0, 3)[:, 0:TT].rearrange("p (n c) -> p n c", c=P)
                for i, w in enumerate((KF, KBW)):
                    for h in range(2):
                        ins = V.tensor_scalar(w[:, :, 64 * h:64 * h + 64], kt[:, :, 64 * h:64 * h + 64],
                                              WK[:, 2 * i + h:2 * i + h + 1], None, ALU.mult)
                ins.then_inc(r_rows, 1)
                per = lambda v: v[:, 0:P * chunks(l)].rearrange("p (n c) -> p n c", c=P)
                wide = lambda w: w.rearrange("p (o c) -> p o c", o=1).to_broadcast([P, chunks(l), P])
                V.tensor_tensor(per(TV), per(TQ), wide(WQ[:, 0]), ALU.mult)
                V.tensor_tensor(per(TMP), per(TQ), wide(WQ[:, 1]), ALU.mult)
                rl(V.memset(SFB[:, :, :, :], 0.0))
                dve.wait_ge(r_u, it + 1)
                for a in range(9):
                    for d, order in enumerate((FWD, BWD)):
                        now, nxt = order[a], order[a + 1]
                        u = psum[:, UBANK[d][now // 4], (now % 4) * P:(now % 4 + 1) * P]
                        for h in range(2):
                            c = slice(64 * h, 64 * h + 64)
                            ins = V.scalar_tensor_tensor(SFB[HALF[h], d, nxt, c], SFB[HALF[h], d, now, c],
                                                         GC[HALF[h], d:d + 1], u[HALF[h], c], ALU.mult, ALU.add)
                    if a < 8:
                        rl(ins)
                    else:
                        ins.then_inc(r_scan, 1)
                for n in range(chunks(l)):
                    dve.wait_ge(r_s, chunks(l) * hp + (n + 1) + RC0[l])
                    if n >= 2:
                        dve.wait_ge(r_omul, chunks(l) * hp + (n - 1) + RC0[l])
                    V.tensor_tensor(SD[:, n % 2].rearrange("p (h c) -> p h c", h=2),
                                    psum[:, 2 * (n % 2):2 * (n % 2) + 2, 0:P], DM[:, :, :], ALU.mult).then_inc(r_sd, 1)
                w = P * chunks(l)
                dve.wait_ge(r_mean, it + 1)
                V.tensor_tensor(RO[:, 0:w], RO[:, 0:w], flat(5, 3)[:, 0:w], ALU.subtract).then_inc(r_cent, 1)
                dve.wait_ge(r_var, it + 1)
                V.tensor_scalar(TMP[:, 0:w], flat(0, 3)[:, 0:w], LN_EPS, None, ALU.add).then_inc(r_eps, 1)
                dve.wait_ge(r_root, it + 1)
                rl(V.reciprocal(TMP[:, 0:w], TMP[:, 0:w]))
                rl(V.tensor_tensor(RO[:, 0:w], RO[:, 0:w], TMP[:, 0:w], ALU.mult))
                V.tensor_tensor(Y2[:, bass.ds(hp + 2, 1), 0:w].rearrange("p a c -> p (a c)"), RO[:, 0:w], TG[:, 0:w],
                                ALU.mult).then_inc(r_done, 1)
                assert n_r[0] == RCH, n_r[0]

        NG = TQ
        QBD = region(14080, 20, P)
        VR2 = region(16640, 17, P)
        BT = region(18816, 15, 64)
        LOG2 = region(19776, 2, 768)
        PT2 = region(21312, 2, 768)
        NMASK = region(22848, 64)
        STAT2 = region(22912, 2, 8)
        PAD = region(0, 6, P)
        rpb_pad = dram("rpb_pad", (2, 6, 15, P))
        rpb_skew = dram("rpb_skew", (2, 6, 64, 15, 64))
        n_zero, n_const, n_self, n_rows, n_norm = [sem(n) for n in ("n_zero", "n_const", "n_self", "n_rows", "n_norm")]
        n_bias, n_pad, n_padded = sem("n_bias"), sem("n_pad"), sem("n_padded")
        ROWS = S // 64
        QU = (ROWS + CTX // 64, ROWS)

        def halves_before(n):
            return 2 * n if n <= ROWS else ROWS + n

        def unit_base(l, hp):
            return QU[l] * hp + (3 * QU[0] * l + U_DONE)

        def half_base(l, hp):
            return halves_before(QU[l]) * hp + (3 * halves_before(QU[0]) * l + 2 * U_DONE)

        def row_start(r):
            return min(max(r - 4, 0), ROWS - 8)

        def parts_of_unit(n):
            return 2 if n < ROWS else 1

        def v_tiles(n):
            if n >= ROWS:
                return [(15, 4), (16, 5)]
            rs = row_start(n)
            first = rs // 2 if rs % 2 == 0 else 8 + (rs - 1) // 2
            return [(first + i, i) for i in range(4)] + [(15, 4), (16, 5)]

        def pad_act(act, l):
            act.wait_ge(n_pad, l + 1)
            for h in range(6):
                act.dma_start(PAD[0:15, h, 48:79], io["na_rpb_2"][l, h]).then_inc(n_bias, 16)
            act.wait_ge(n_bias, 16 * 6 * (l + 1))
            act.dma_start(rpb_pad[l].rearrange("h a k -> a h k"), PAD[0:15]).then_inc(n_padded, 16)
            act.wait_ge(n_padded, 16 * (7 * l + 1))
            for h in range(6):
                src = rpb_pad[l, h]
                act.dma_start(rpb_skew[l, h].rearrange("q a c -> a q c"),
                              bass.AP(tensor=src.tensor, offset=src.offset + 63, ap=[[P, 15], [-1, 64], [1, 64]])
                              ).then_inc(n_padded, 16)
            act.wait_ge(n_padded, 16 * 7 * (l + 1))

        def nat_pe(pe, l):
            with pe.Fori(0, 3) as hp:
                it = hp + 3 * l
                m = 4 * hp + (12 + 32 * l)
                u0, h0 = unit_base(l, hp), half_base(l, hp)
                pe.wait_ge(u_evac, u0)
                for j in range(4):
                    p_slot(pe, l, m + j, j % 2, j < 2)
                pe.wait_ge(p_evac, m + 4 + 2)
                for t in range(17):
                    c0 = P * t if t < 8 else 64 + P * (t - 8) if t < 15 else S + P * (t - 15)
                    ins = nc.tensor.transpose(psum[:, t // 4, (t % 4) * P:(t % 4 + 1) * P], TV[:, c0:c0 + P], ident[:, :])
                ins.then_inc(v_turned, 1)
                pe.wait_ge(n_rows, it + 1)

                def scores(n):
                    b = n % 2
                    if n >= 2:
                        pe.wait_ge(u_probs, h0 + halves_before(n - 1))
                    if n < ROWS:
                        nc.tensor.matmul(psum[:, 2 * b, :], QBD[:, n], TK[:, 64 * row_start(n):64 * row_start(n) + 512],
                                         start=True, stop=True)
                    nc.tensor.matmul(psum[:, 2 * b + 1, 0:CTX], QBD[:, n], TK[:, S:TT], start=True, stop=True
                                     ).then_inc(u_scores, 1)

                def turn_p(n):
                    pe.wait_ge(n_norm, u0 + (n + 1) - U_DONE)
                    pe.wait_ge(u_pt, u0 + n)
                    for _, i in v_tiles(n):
                        ins = nc.tensor.transpose(psum[:, 4 + i // 4, (i % 4) * P:(i % 4 + 1) * P],
                                                  LOG2[:, n % 2, i * P:(i + 1) * P], ident[:, :])
                    ins.then_inc(u_turned, 1)

                def outputs(n):
                    pe.wait_ge(u_pt, u0 + (n + 1))
                    if n >= 2:
                        pe.wait_ge(u_evac, u0 + (n - 1))
                    tiles = v_tiles(n)
                    for a, (t, i) in enumerate(tiles):
                        ins = nc.tensor.matmul(psum[:, 6 + n % 2, 0:P], VR2[:, t], PT2[:, n % 2, i * P:(i + 1) * P],
                                               start=(a == 0), stop=(a == len(tiles) - 1))
                    ins.then_inc(u_out, 1)

                scores(0)
                scores(1)
                for n in range(QU[l]):
                    turn_p(n)
                    if n + 2 < QU[l]:
                        scores(n + 2)
                    outputs(n)

        def nat_act(act, l):
            act.dma_start(NMASK[:, :], io["c_nmask"]).then_inc(n_const, 16)
            with act.Fori(0, 3) as hp:
                it = hp + 3 * l
                m = 4 * hp + (12 + 32 * l)
                u0, h0 = unit_base(l, hp), half_base(l, hp)
                act.wait_ge(u_evac, u0)
                act.dma_start(BT.rearrange("p a c -> p (a c)"), rpb_skew[l].rearrange("h q a c -> (h q) (a c)")[bass.ds(hp * P, P), :]
                              ).then_inc(n_const, 16)
                p_take(act, l, m, 0, True, TK)
                p_take(act, l, m + 1, 1, True, TV)
                act.wait_ge(slot_used, SLOT_L3[l] + (m + 2 - 32 * l) + 3)
                act.wait_ge(n_zero, l + 1)
                for h in range(2):
                    ins = nc.scalar.activation(QBD[HALF[h], 0:QU[l], 64 * h:64 * h + 64],
                                               flat(0, 3)[HALF[h], 0:64 * QU[l]].rearrange("p (r c) -> p r c", c=64),
                                               ACT.Copy, scale=SCALE)
                ins.then_inc(p_evac, 1)
                p_take(act, l, m + 3, 1, False, NG, ACT.Silu)
                for n in range(QU[l]):
                    b, hb = n % 2, h0 + halves_before(n)
                    act.wait_ge(u_negmax, u0 + (n + 1))
                    if n < ROWS:
                        nc.scalar.activation(LOG2[:, b, 0:512], LOG2[:, b, 0:512], ACT.Exp, bias=STAT2[:, b, 4:5],
                                             accum_out=STAT2[:, b, 0:1]).then_inc(u_probs, 1)
                    nc.scalar.activation(LOG2[:, b, 512:768], psum[:, 2 * b + 1, 0:CTX], ACT.Exp, bias=STAT2[:, b, 4:5],
                                         accum_out=STAT2[:, b, 1:2]).then_inc(u_probs, 1)
                    act.wait_ge(u_turned, u0 + (n + 1))
                    if n >= 2:
                        act.wait_ge(u_out, u0 + (n - 1))
                    c0 = 0 if n < ROWS else 512
                    nc.scalar.copy(PT2[:, b, c0:768], flat(4, 2)[:, c0:768]).then_inc(u_pt, 1)

        def nat_dve(dve, l):
            V = nc.vector
            SELF = 1 + 2 * ROWS + (QU[l] - ROWS)
            self0 = 3 * (1 + 2 * ROWS + QU[0] - ROWS) * l
            V.memset(QBD[:, :, :], 0.0).then_inc(n_zero, 1)
            with dve.Fori(0, 3) as hp:
                it = hp + 3 * l
                u0, h0 = unit_base(l, hp), half_base(l, hp)
                n_s = [0]

                def own(ins):
                    n_s[0] += 1
                    ins.then_inc(n_self, 1)
                    dve.wait_ge(n_self, SELF * hp + (self0 + n_s[0]))

                dve.wait_ge(n_const, 16 * it + (16 + 16 * (l + 1)))
                own(V.tensor_tensor(BT[:, :, :], BT[:, :, :], NMASK.rearrange("p (o c) -> p o c", o=1).to_broadcast([P, 15, 64]),
                                    ALU.add))
                dve.wait_ge(v_turned, it + (1 + VT_DONE))
                V.tensor_copy(VR2.rearrange("p a c -> p (a c)"), flat(0, 5)[:, 0:17 * P]).then_inc(n_rows, 1)

                def logits(n):
                    b, hb = n % 2, h0 + halves_before(n)
                    dve.wait_ge(u_scores, u0 + (n + 1))
                    if n >= 2:
                        dve.wait_ge(u_turned, u0 + (n - 1))
                    V.memset(STAT2[:, b, 7:8], 0.0)
                    if n < ROWS:
                        dr = row_start(n) - n + 7
                        V.tensor_tensor_reduce(LOG2[:, b, 0:512], psum[:, 2 * b, :],
                                               BT[:, dr:dr + 8, :].rearrange("p a c -> p (a c)"),
                                               1.0, -3e38, ALU.add, ALU.max, accum_out=STAT2[:, b, 2:3]).then_inc(u_logits, 1)
                    V.tensor_reduce(STAT2[:, b, 3:4], psum[:, 2 * b + 1, 0:CTX], AX.X, ALU.max).then_inc(u_logits, 1)
                    dve.wait_ge(u_logits, h0 + halves_before(n + 1))
                    if n < ROWS:
                        V.tensor_scalar(STAT2[:, b, 4:5], STAT2[:, b, 3:4], STAT2[:, b, 2:3], -1.0, ALU.max,
                                        ALU.mult).then_inc(u_negmax, 1)
                    else:
                        V.tensor_scalar(STAT2[:, b, 4:5], STAT2[:, b, 3:4], -1.0, None, ALU.mult).then_inc(u_negmax, 1)

                def normalise(n):
                    b = n % 2
                    dve.wait_ge(u_probs, h0 + halves_before(n + 1))
                    total = STAT2[:, b, 1:2]
                    if n < ROWS:
                        own(V.tensor_tensor(STAT2[:, b, 5:6], STAT2[:, b, 0:1], STAT2[:, b, 1:2], ALU.add))
                        total = STAT2[:, b, 5:6]
                    own(V.reciprocal(STAT2[:, b, 6:7], total))
                    c0 = 0 if n < ROWS else 512
                    V.tensor_scalar(LOG2[:, b, c0:768], LOG2[:, b, c0:768], STAT2[:, b, 6:7], None, ALU.mult).then_inc(n_norm, 1)

                def evacuate(n):
                    dve.wait_ge(u_out, u0 + (n + 1))
                    for h in range(2):
                        ins = V.tensor_tensor(Y2[HALF[h], bass.ds(hp + 5, 1), 64 * n:64 * n + 64].rearrange("p a c -> p (a c)"),
                                              psum[HALF[h], 6 + n % 2, 64 * h:64 * h + 64],
                                              NG[HALF[h], 64 * n:64 * n + 64], ALU.mult)
                    ins.then_inc(u_evac, 1)

                logits(0)
                for n in range(QU[l]):
                    if n + 1 < QU[l]:
                        logits(n + 1)
                    normalise(n)
                    if n > 0:
                        evacuate(n - 1)
                evacuate(QU[l] - 1)
                assert n_s[0] == SELF

        VH, VB, VC, VZ, VO = (region(10240 + i * 1290, 1284) for i in range(5))
        VU = region(10240 + 5 * 1290, 1284)
        CW = region(10240 + 6 * 1290, 2, 4)
        CWC = region(10240 + 6 * 1290 + 8, 4)
        v_const, v_chain, v_done = sem("v_const"), sem("v_chain"), sem("v_done")
        V_CHAIN = 7

        def conv_segs(l):
            return ((0, 0, S), (S + 2, S, CTX))[0:2 - l]

        def conv_pe(pe, l):
            with pe.Fori(0, 2) as c:
                for j in range(4):
                    p_slot(pe, l, 4 * c + (24 + 32 * l) + j, j % 2, False)

        def conv_act(act, l):
            slow = dict(allow_slow_non_contiguous=True)
            for k in range(3):
                act.dma_start(CW[:, :, k], io["conv_w_2"][l, k].rearrange("(c p) -> p c", p=P), **slow).then_inc(v_const, 16)
            act.dma_start(CW[:, :, 3], io["conv_b_2"][l].rearrange("(c p) -> p c", p=P), **slow).then_inc(v_const, 16)
            with act.Fori(0, 2) as c:
                act.wait_ge(v_done, c + (2 * l + 1))
                for j, (dst, f) in enumerate(((VH, ACT.Copy), (VB, ACT.Copy), (VC, ACT.Copy), (VZ, ACT.Silu))):
                    p_take(act, l, 4 * c + (24 + 32 * l) + j, j % 2, False, dst, f)

        def conv_dve(dve, l):
            V = nc.vector
            if l == 0:
                dve.sem_inc(v_done, 1)
            V.memset(VU[:, :], 0.0).then_inc(v_chain, 1)
            dve.wait_ge(v_const, 64 * (l + 1))
            with dve.Fori(0, 2) as c:
                n_v = [0]

                def own(ins):
                    n_v[0] += 1
                    ins.then_inc(v_chain, 1)
                    dve.wait_ge(v_chain, V_CHAIN * c + (1 + (1 + 2 * V_CHAIN) * l + n_v[0]))

                own(V.tensor_copy(CWC, CW[:, bass.ds(c, 1), :].rearrange("p a c -> p (a c)")))
                dve.wait_ge(p_evac, 4 * c + (24 + 32 * l + 4 + 2))
                n_seg = len(conv_segs(l))
                for i, (u, y, n) in enumerate(conv_segs(l)):
                    ins = V.tensor_tensor(VU[:, u + 1:u + 1 + n], VC[:, y:y + n], VH[:, y:y + n], ALU.mult)
                own(ins)
                w = S if l == 1 else S + 2 + CTX
                own(V.tensor_scalar(VO[:, 0:w], VU[:, 0:w], CWC[:, 0:1], CWC[:, 3:4], ALU.mult, ALU.add))
                for k in (1, 2):
                    own(V.scalar_tensor_tensor(VO[:, 0:w], VU[:, k:k + w], CWC[:, k:k + 1], VO[:, 0:w], ALU.mult, ALU.add))
                for i, (u, y, n) in enumerate(conv_segs(l)):
                    ins = V.tensor_tensor(VO[:, u:u + n], VO[:, u:u + n], VB[:, y:y + n], ALU.mult)
                own(ins)
                own(V.memset(CWC, 0.0))
                for i, (u, y, n) in enumerate(conv_segs(l)):
                    ins = V.tensor_tensor(Y2[:, bass.ds(c, 1), y:y + n].rearrange("p a c -> p (a c)"), VO[:, u:u + n],
                                          VZ[:, y:y + n], ALU.mult)
                ins.then_inc(v_done, 1)
                assert n_v[0] == V_CHAIN, n_v[0]

        F_GATE = region(8192, 2, 1024)
        F_LN = region(10240, 2, 1024)
        F_SQ = region(12288, 1024)
        F_ST2 = region(13312, 2, 8)
        ALPHA = 4.0 ** 0.25
        f_chain = sem("f_chain")
        FIVE = (((0, 1, 2, 3), (4, 5, 6, 7), (8, 9)), ((0, 1, 2, 3), (4, 5, 6, 7)))

        def ln_rows(tok, con):
            return lambda t: tok[t * P:(t + 1) * P, :] if t < NT else con[(t - NT) * P:(t - NT + 1) * P, :]

        def ln_act(act, l, base, slot0, xrows, orows):
            passes = FIVE[l]
            tiles = [t for p in passes for t in p]
            for i in range(2):
                act.dma_start(F_GATE[:, i], spread_rows(mod_rows[l, i, 2048:3072])).then_inc(f_const, 16)
            act.dma_start(F_LN[:, 0], spread_rows(io["ln_g_2"][l])).then_inc(f_const, 16)
            act.dma_start(F_LN[:, 1], spread_rows(io["ln_b_2"][l])).then_inc(f_const, 16)
            for n in range(2):
                act.dma_start(F_X[:, n], xrows(tiles[n])).then_inc(f_loaded[n], 16)
            for n, t in enumerate(tiles):
                b, m = n % 2, base + n
                act.wait_ge(f_chain, 4 * (m - F_DONE) + 2)
                nc.scalar.activation(F_SQ[:, :], F_T[:, b], ACT.Square, bias=F_ST2[:, b, 1:2],
                                     accum_out=F_ST2[:, b, 2:3]).then_inc(f_square, 1)
                act.wait_ge(f_var, m + 1)
                nc.scalar.activation(F_ST2[:, b, 4:5], F_ST2[:, b, 3:4], ACT.Sqrt).then_inc(f_root, 1)
                act.wait_ge(f_sum, m + 1)
                act.dma_start(orows(t), F_T[:, b]).then_inc(f_stored[b], 16)
                if n + 2 < len(tiles):
                    act.dma_start(F_X[:, b], xrows(tiles[n + 2])).then_inc(f_loaded[b], 16)
            for b in range(2):
                act.wait_ge(f_stored[b], 16 * ((base + len(tiles)) // 2))

        def ln_dve(dve, l, base, slot0):
            V = nc.vector
            passes = FIVE[l]
            dve.wait_ge(f_const, 16 * (FC_DONE + 4 * (l + 1)))
            n = 0
            for p, ts in enumerate(passes):
                dve.wait_ge(slot_used, slot0 + KT * (p + 1) + 2)
                for j, t in enumerate(ts):
                    b, m = n % 2, base + n
                    k = 4 * (m - F_DONE)
                    st = F_ST2[:, b]
                    if n >= 2:
                        dve.wait_ge(f_stored[b], 16 * (m // 2))
                    V.tensor_tensor(F_T[:, b], ps_tile(j), F_GATE[:, 0 if t < NT else 1], ALU.mult).then_inc(f_scaled, 1)
                    dve.wait_ge(f_scaled, m + 1)
                    dve.wait_ge(f_loaded[b], 16 * (m // 2 + 1))
                    V.scalar_tensor_tensor(F_T[:, b], F_X[:, b], ALPHA, F_T[:, b], ALU.mult, ALU.add,
                                           accum_out=st[:, 0:1]).then_inc(f_chain, 1)
                    dve.wait_ge(f_chain, k + 1)
                    V.tensor_scalar(st[:, 1:2], st[:, 0:1], -1.0 / D, None, ALU.mult).then_inc(f_chain, 1)
                    dve.wait_ge(f_square, m + 1)
                    V.tensor_scalar(st[:, 3:4], st[:, 2:3], 1.0 / D, LN_EPS, ALU.mult, ALU.add).then_inc(f_var, 1)
                    dve.wait_ge(f_root, m + 1)
                    V.reciprocal(st[:, 5:6], st[:, 4:5]).then_inc(f_rstd, 1)
                    dve.wait_ge(f_rstd, m + 1)
                    V.tensor_scalar(F_T[:, b], F_T[:, b], st[:, 1:2], st[:, 5:6], ALU.add, ALU.mult).then_inc(f_chain, 1)
                    dve.wait_ge(f_chain, k + 3)
                    V.tensor_tensor(F_T[:, b], F_T[:, b], F_LN[:, 0], ALU.mult).then_inc(f_chain, 1)
                    dve.wait_ge(f_chain, k + 4)
                    V.tensor_tensor(F_T[:, b], F_T[:, b], F_LN[:, 1], ALU.add).then_inc(f_sum, 1)
                    n += 1

        G_X, G_C = region(8192 + 6152 + 16, 2, 8), region(8192 + 6152 + 32, 2, 8)
        t_gain = sem("t_gain")
        XROWS = (rows(x2), rows(x3))
        CROWS = (rows(io["ctx_2"][0]), rows(xc3))
        LNX = (ln_rows(x2, io["ctx_2"][0]), ln_rows(x3, xc3))
        LNO = (ln_rows(x3, xc3), ln_rows(out.rearrange("b s d -> (b s) d"), None))

        def hybrid_pe(pe, l):
            g = STAGES_DONE + 7 * l
            m_pe(pe, l)
            stage_end(pe, g + 1)
            t_pe(pe, T_DONE + 10 * l, NT + 2)
            stage_end(pe, g + 2)
            ret_pe(pe, l)
            stage_end(pe, g + 3)
            nat_pe(pe, l)
            stage_end(pe, g + 4)
            conv_pe(pe, l)
            stage_end(pe, g + 5)
            stage_end(pe, g + 6)
            r_pe(pe, SLOT_L3[l] + 32, FIVE[l], f_scaled, F_DONE + 10 * l)
            stage_end(pe, g + 7)

        def hybrid_act(act, l):
            g = STAGES_DONE + 7 * l
            m_act(act, l)
            pad_act(act, l)
            stage_end(act, g + 1)
            for i, gain in enumerate((G_X, G_C)):
                for j, c0 in enumerate((1024, 0)):
                    act.dma_start(gain[:, j], mod_rows[l, i, c0:c0 + 1024].rearrange("(k p) -> p k", p=P),
                                  allow_slow_non_contiguous=True).then_inc(const_loaded, 16)
            act.wait_ge(t_gain, 2 * (l + 1))
            t_act(act, T_DONE + 10 * l, NT, XROWS[l], False, G_X, 0)
            t_act(act, T_DONE + 10 * l + NT, 2, CROWS[l], False, G_C, S)
            stage_end(act, g + 2)
            if l == 0:
                act.sem_inc(p_evac, 2)
            ret_act(act, l)
            stage_end(act, g + 3)
            nat_act(act, l)
            stage_end(act, g + 4)
            conv_act(act, l)
            stage_end(act, g + 5)
            y_act(act, Y_DONE + KT * l, Y2, False, (TT, S)[l])
            stage_end(act, g + 6)
            ln_act(act, l, F_DONE + 10 * l, SLOT_L3[l] + 32, LNX[l], LNO[l])
            stage_end(act, g + 7)

        def hybrid_dve(dve, l):
            g = STAGES_DONE + 7 * l
            nc.vector.memset(PAD[0:15, :, :], 0.0).then_inc(n_pad, 1)
            m_dve(dve, l)
            stage_end(dve, g + 1)
            dve.wait_ge(const_loaded, 16 * (CONST_DONE + 4 * (l + 1)))
            for gain in (G_X, G_C):
                nc.vector.tensor_scalar(gain[:, 0], gain[:, 0], 1.0, None, ALU.add).then_inc(t_gain, 1)
            dve.wait_ge(t_gain, 2 * (l + 1))
            t_dve(dve, T_DONE + 10 * l, NT, False, G_X, 0)
            t_dve(dve, T_DONE + 10 * l + NT, 2, False, G_C, S)
            stage_end(dve, g + 2)
            ret_dve(dve, l)
            stage_end(dve, g + 3)
            nat_dve(dve, l)
            stage_end(dve, g + 4)
            conv_dve(dve, l)
            stage_end(dve, g + 5)
            y_dve(dve, Y_DONE + KT * l, Y2, False, (TT, S)[l])
            stage_end(dve, g + 6)
            ln_dve(dve, l, F_DONE + 10 * l, SLOT_L3[l] + 32)
            stage_end(dve, g + 7)

        block = ctx.enter_context(nc.Block())

        @block.sync
        def _(sp):
            def load(par, n, dst, src):
                sp.wait_ge(slot_split, n + 1)
                sp.dma_start(dst, src).then_inc(slot_loaded[par], 16)

            def load_t(par, n, w, col):
                load(par, n, w_raw[:, par].rearrange("p (k c) -> p k c", k=KT),
                     w.rearrange("(k p) c -> p k c", p=P)[:, :, bass.ds(col, P)])

            def load_rows(slot0, w, c0=0):
                with sp.Fori(0, KT // 2) as k2:
                    for par in range(2):
                        load(par, 2 * k2 + (slot0 + par), w_raw[:, par], w[bass.ds(k2 * 256 + par * P, P), c0:c0 + 1024])

            w1 = io["attn_w_in"][0]
            with sp.Fori(1, HP + 1) as hp1:
                for j in range(L1_PER_HP):
                    load_t(j % 2, L1_PER_HP * hp1 + (j - L1_PER_HP), w1, slot_col(j, 0) + (hp1 * P - P))
            for th in range(2):
                load_rows(SLOT_F1 + KT * th, io["attn_w_out"][0])
            for i, (w, c0) in enumerate(((io["ssm_w_in"][0], 0), (io["ssm_w_in"][0], 1024),
                                         (io["ssm_w_glu"][0], 0), (io["ssm_w_out"][0], 0))):
                for th in range(2):
                    load_rows(SLOT_U + KT * (2 * i + th), w, c0)
            for l in range(2):
                w, b = io["w_in_2"][l], SLOT_L3[l]
                for first, count, cols, step in ((0, 3, (0, 384, 1536, 1920), 12), (12, 3, (768, 1152, 2304, 2688), 12),
                                                 (24, 2, (3072, 3328, 3584, 3840), 8)):
                    with sp.Fori(0, count) as i:
                        for j, col in enumerate(cols):
                            load_t(j % 2, 4 * i + (b + first + j), w, i * P + col)
                for p in range(3 - l):
                    load_rows(b + 32 + KT * p, io["w_out_2"][l])

        @block.gpsimd
        def _(pool):
            nc.gpsimd.memset(one[:, :], 1.0).then_inc(one_set, 1)
            pool.wait_ge(one_set, 1)
            pool.sem_inc(slot_split, 2)
            with pool.Fori(0, N_SLOTS // 2) as m:
                for par in range(2):
                    pool.wait_ge(slot_loaded[par], 16 * m + 16)
                    pool.wait_ge(slot_used, 2 * m + (par + 1))
                    nc.gpsimd.tensor_tensor(w_hi[:, par], w_raw[:, par], one[:, 0:1].to_broadcast([P, 1024]),
                                            ALU.mult).then_inc(slot_hi, 1)
                    pool.wait_ge(slot_hi, 2 * m + (par + 1))
                    nc.gpsimd.tensor_tensor(w_lo[:, par], w_raw[:, par], w_hi[:, par].bitcast(F32),
                                            ALU.subtract).then_inc(slot_split, 1)

        @block.tensor
        def _(pe):
            pe.sem_inc(slot_used, 2)
            pe.wait_ge(k_load, 16 * K_LOADS)
            for ri in range(2):
                for q in range(8):
                    ins = nc.tensor.transpose(psum[:, 2 * ri + q // 4, (q % 4) * P:(q % 4 + 1) * P],
                                              KCL[:, ri, q], ident[:, :])
            ins.then_inc(k_turned, 1)
            for ri in range(2):
                pe.wait_ge(k_b, ri + 1)
                for bt in range(8):
                    n = 8 * ri + bt
                    if n >= 2:
                        pe.wait_ge(k_bcopy, n - 1)
                    for i in range(4):
                        ins = nc.tensor.transpose(psum[:, 4 + n % 2, i * P:(i + 1) * P],
                                                  KBP[:, 4 * bt + i].rearrange("p s c -> p (s c)"), ident[:, :])
                    ins.then_inc(k_bt, 1)
            pe.wait_ge(k_cp, 1)
            for bt in range(8):
                if bt >= 2:
                    pe.wait_ge(k_kk, 2 * (bt - 1))
                for i in range(4):
                    for g2 in range(2):
                        for ri in range(2):
                            gp = 4 * bt + i
                            ins = nc.tensor.matmul(psum[0:16, 2 * (bt % 2) + g2, i * P:(i + 1) * P],
                                                   KBB[64 * g2:64 * g2 + 64, ri, gp],
                                                   KCP[64 * g2:64 * g2 + 64, ri, gp, 0:P],
                                                   start=(ri == 0), stop=(ri == 1))
                ins.then_inc(k_conv, 1)
            stage_end(pe, 1)

            pe.wait_ge(const_loaded, 16 * 3)
            pe.wait_ge(b_copied, 1)
            for g in range(3):
                ins = nc.tensor.matmul(psum[0:16, 4 + g, 0:384], relb[0:33, :], onehot[0:33, g * 384:(g + 1) * 384],
                                       start=True, stop=True)
            ins.then_inc(b_spread, 1)
            t_pe(pe, 0, NT)
            stage_end(pe, 2)

            with pe.Fori(0, HP) as hp:
                for j in range(L1_PER_HP):
                    pe.wait_ge(g_evac[j % 2], 5 * hp + (j // 2 + 1))
                    mul_t(pe, L1_PER_HP * hp + j, j % 2, (2 * (j % 2), 2 * (j % 2) + 1), ((0, 512), (512, 512)))
                pe.wait_ge(g_evac[0], 5 * hp + 5 + 1)
                pe.wait_ge(g_evac[1], 5 * hp + 5 + 1)

                def scores(n):
                    g, u = UNITS[n]
                    if n >= 2:
                        pe.wait_ge(u_logits, 2 * NU * hp + 2 * (n - 1))
                    kt = key_tiles(g, u)
                    for h in range(2):
                        ins = nc.tensor.matmul(psum[:, 2 * (n % 2) + h, 0:P * len(kt)],
                                               QKV[64 * h:64 * h + 64, 3 * g, u * P:(u + 1) * P],
                                               QKV[64 * h:64 * h + 64, 3 * g + 1, kt[0] * P:(u + 1) * P],
                                               start=True, stop=True)
                    ins.then_inc(u_scores, 1)

                def turn_v(g):
                    if g > 0:
                        pe.wait_ge(u_pt, NU * hp + 8 * g)
                    for half in range(2):
                        bank = 5 + half
                        for i in range(4):
                            t = 4 * half + i
                            ins = nc.tensor.transpose(psum[:, bank, i * P:(i + 1) * P],
                                                      QKV[:, 3 * g + 2, t * P:(t + 1) * P], ident[:, :])
                        ins.then_inc(v_turned, 1)

                def turn_p(n):
                    g, u = UNITS[n]
                    nk = len(key_tiles(g, u))
                    pe.wait_ge(u_probs, 2 * NU * hp + 2 * n + 2)
                    if n % 8 < 2:
                        pe.wait_ge(v_rows[n % 2], 3 * hp + g + 1)
                    else:
                        pe.wait_ge(u_pt, NU * hp + n - 1)
                    for h in range(2):
                        for i in range(nk):
                            ins = nc.tensor.transpose(psum[:, 5 + n % 2, (2 * h + i) * P:(2 * h + i + 1) * P],
                                                      LOG[:, n % 2, h * 256 + i * P:h * 256 + (i + 1) * P],
                                                      ident[:, :])
                    ins.then_inc(u_turned, 1)

                def outputs(n):
                    g, u = UNITS[n]
                    kt = key_tiles(g, u)
                    pe.wait_ge(u_pt, NU * hp + n + 1)
                    if n % 8 == 0:
                        pe.wait_ge(v_rows[0], 3 * hp + g + 1)
                        pe.wait_ge(v_rows[1], 3 * hp + g + 1)
                    if n >= 2:
                        pe.wait_ge(u_evac, NU * hp + n - 1)
                    for h in range(2):
                        for i, t in enumerate(kt):
                            nc.tensor.matmul(psum[64 * h:64 * h + 64, OB(n), 0:P],
                                             VROW[:, t, 64 * h:64 * h + 64],
                                             PT[:, n % 2, (2 * h + i) * P:(2 * h + i + 1) * P],
                                             start=(i == 0), stop=(i == len(kt) - 1))
                    pe.wait_ge(u_wide, NU * hp + n + 1)
                    for c in range(2):
                        ins = nc.tensor.transpose(psum[:, OB(n), (c + 1) * P:(c + 2) * P],
                                                  WIDE[:, n % 2, c * P:(c + 1) * P], ident[:, :])
                    ins.then_inc(u_out, 1)

                for g in range(3):
                    turn_v(g)
                    for n in range(8 * g, 8 * g + 8):
                        if n == 8 * g:
                            scores(n)
                            scores(n + 1)
                        turn_p(n)
                        if n + 2 < 8 * g + 8:
                            scores(n + 2)
                        outputs(n)
            stage_end(pe, 3)
            stage_end(pe, 4)
            r_pe(pe, SLOT_F1, HALVES, f_scaled, 0)
            stage_end(pe, 5)
            t_pe(pe, 8, NT)
            stage_end(pe, 6)
            r_pe(pe, SLOT_U, HALVES, u_copied, 0)
            pe.wait_ge(u_copied, 8)
            r_pe(pe, SLOT_U + 2 * KT, HALVES, z_scaled, 0)
            stage_end(pe, 7)

            def turn_pair(gp, n):
                if n >= 2:
                    pe.wait_ge(s_ut, n - 1)
                for g2 in range(2):
                    ins = nc.tensor.transpose(psum[:, n % 2, g2 * P:(g2 + 1) * P], U[:, 2 * gp + g2], ident[:, :])
                ins.then_inc(s_turned, 1)

            turn_pair(0, 0)
            for gp in range(G2):
                if gp + 1 < G2:
                    turn_pair(gp + 1, gp + 1)
                pe.wait_ge(s_ut, gp + 1)
                pe.wait_ge(s_loaded[gp % 2], 16 * (gp // 2 + 1))
                if gp >= 2:
                    pe.wait_ge(s_out, gp - 1)
                for ri in range(2):
                    for g2 in range(2):
                        ins = nc.tensor.matmul(psum[64 * g2:64 * g2 + 64, 2 + gp % 2, ri * P:(ri + 1) * P],
                                               SP_RING[:, gp % 2, ri * P + 64 * g2:ri * P + 64 * g2 + 64],
                                               UT[:, gp % 2, g2 * P:(g2 + 1) * P], start=True, stop=True)
                ins.then_inc(s_mul, 1)
            turn_pair(0, G2)
            pe.wait_ge(q_dve, Q_OPS)
            for gp in range(G2):
                n = G2 + gp
                if gp + 1 < G2:
                    turn_pair(gp + 1, n + 1)
                pe.wait_ge(s_ut, n + 1)
                pe.wait_ge(s_loaded[gp % 2], 16 * (16 + 2 * (gp // 2) + 2))
                if gp >= 2:
                    pe.wait_ge(s_out, n - 1)
                for g2 in range(2):
                    o = psum[:, 4 + 2 * (gp % 2) + g2, 0:P]
                    nc.tensor.matmul(o, UT[:, gp % 2, g2 * P:(g2 + 1) * P],
                                     SP_RING[:, gp % 2, g2 * P:(g2 + 1) * P], start=True, stop=False)
                    for ri in range(2):
                        ins = nc.tensor.matmul(o, ST[64 * g2:64 * g2 + 64, gp, ri, 0:P],
                                               SP_RING[64 * g2:64 * g2 + 64, gp % 2, 256 + ri * P:256 + (ri + 1) * P],
                                               start=False, stop=(ri == 1))
                ins.then_inc(s_mul, 1)
            stage_end(pe, 8)
            x_pe(pe, 0, YR, NT)
            stage_end(pe, 9)
            r_pe(pe, SLOT_U + 4 * KT, HALVES, h_sum, 0)
            stage_end(pe, 10)
            x_pe(pe, 8, YR, NT)
            stage_end(pe, 11)
            r_pe(pe, SLOT_U + 6 * KT, HALVES, f_scaled, 8)
            stage_end(pe, 12)
            for l in range(2):
                hybrid_pe(pe, l)

        @block.scalar
        def _(act):
            act.dma_start(ident[:, :], io["c_ident"]).then_inc(k_load, 16)
            halves = lambda g2: slice(64 * g2, 64 * g2 + 64)
            slow = dict(allow_slow_non_contiguous=True)
            for g2 in range(2):
                for i, name in enumerate(("ssm_a_re", "ssm_a_im")):
                    src = io[name][0].rearrange("(gp g) p -> g p gp", g=2)[g2]
                    act.dma_start(KA[halves(g2), i], src, **slow).then_inc(k_load, 16)
                dt = io["ssm_log_dt"][0]
                act.dma_start(KA[halves(g2), 2], bass.AP(tensor=dt.tensor, offset=dt.offset + g2, ap=[[0, 64], [2, 32]]),
                              **slow).then_inc(k_load, 16)
                for i, name in enumerate(("ssm_b_re", "ssm_b_im")):
                    src = io[name][0].rearrange("(gp g) p c -> g p gp c", g=2)[g2]
                    act.dma_start(KB[halves(g2), i], src).then_inc(k_load, 16)
                for i, name in enumerate(("ssm_c_re", "ssm_c_im")):
                    src = io[name][0].rearrange("(q g) c p -> (g c) q p", g=8)
                    act.dma_start(KCL[:, i, :, 64 * g2:64 * g2 + 64], src).then_inc(k_load, 16)
            d = io["ssm_d"][0]
            act.dma_start(KD[0:16], bass.AP(tensor=d.tensor, offset=d.offset, ap=[[0, 16], [16, 64], [1, 16]])).then_inc(k_load, 16)
            act.wait_ge(k_chain, 1)
            for i in range(16):
                act.dma_start(k_mat[:, 4 * i:4 * i + 4, 0:P], KZ.rearrange("p (g c) -> p g c", g=4)).then_inc(k_stored, 16)
            act.wait_ge(k_stored, 16 * 16)
            act.wait_ge(k_arg, 1)
            nc.scalar.activation(KA[:, 8:10].rearrange("p a b -> p (a b)"), KA[:, 6:8].rearrange("p a b -> p (a b)"),
                                 ACT.Sin).then_inc(k_trig, 1)
            act.wait_ge(k_turned, 1)
            for ri in range(2):
                for g2 in range(2):
                    for h in range(2):
                        nc.scalar.copy(KC[halves(g2), ri, 16 * h:16 * h + 16, :],
                                       psum[halves(g2), 2 * ri + h, :].rearrange("p (x g c) -> p g x c", g=2, c=16)[:, g2]
                                       ).then_inc(k_c, 1)
            for n in range(16):
                ri, bt = n // 8, n % 8
                act.wait_ge(k_bt, n + 1)
                if n >= 2:
                    act.wait_ge(k_bst[n % 2], 16 * (n // 2))
                nc.scalar.copy(KBT[:, n % 2], psum[:, 4 + n % 2, :]).then_inc(k_bcopy, 1)
                act.wait_ge(k_bcopy, n + 1)
                act.dma_start(b_mat[4 * bt:4 * bt + 4, :, ri * P:(ri + 1) * P].rearrange("g p c -> p g c"),
                              KBT[:, n % 2].rearrange("p (g c) -> p g c", g=4)).then_inc(k_bst[n % 2], 16)
            act.wait_ge(k_cp, 1)
            for ri in range(2):
                act.dma_start(c_mat[:, :, ri * P:(ri + 1) * P].rearrange("g p c -> p g c"),
                              KCP[:, ri, :, 16:144]).then_inc(k_stored, 16)
                act.dma_start(q_pow[:, ri * 512:(ri + 1) * 512], KQ[:, ri].rearrange("p a b -> p (a b)")).then_inc(k_stored, 16)
            for bt in range(8):
                act.wait_ge(k_kk, 2 * bt + 2)
                for g2 in range(2):
                    act.dma_start(k_mat[:, 8 * bt:8 * bt + 8, P:2 * P].rearrange("c (a g) k -> g c a k", g=2)[g2],
                                  KK[0:16, bt % 2, g2].rearrange("p (a k) -> p a k", a=4)).then_inc(k_kst[bt % 2], 16)
            for b in range(2):
                act.wait_ge(k_bst[b], 16 * 8)
                act.wait_ge(k_kst[b], 16 * 8)
            act.wait_ge(k_stored, 16 * 20)
            for s_ in range(8):
                for g2 in range(2):
                    act.dma_start(m_mat[:, 16 * s_:16 * s_ + 16, g2 * P:(g2 + 1) * P].rearrange("a c k -> c a k"),
                                  k_mat[:, :, 16 + 16 * s_:144 + 16 * s_].rearrange("c (a g) k -> g c a k", g=2)[g2]
                                  ).then_inc(k_stored, 16)
            act.wait_ge(k_stored, 16 * 36)
            stage_end(act, 1)

            act.dma_start(onehot[0:33, :], io["c_onehot"]).then_inc(const_loaded, 16)
            act.dma_start(relb[0:32, :], io["rel_bias"]).then_inc(const_loaded, 16)
            act.dma_start(T_GAIN[:, 0, :], io["attn_pre_norm"].rearrange("a (k p) -> p (a k)", p=P),
                          allow_slow_non_contiguous=True).then_inc(const_loaded, 16)
            t_act(act, 0, NT, t_src_rows(x_in, False), True, T_GAIN, 0)
            act.wait_ge(b_copied, 3)
            act.dma_start(bias_rows, spread[0:16].rearrange("p a b -> p (a b)")).then_inc(b_stored, 16)
            act.wait_ge(b_stored, 16)
            for g in range(2):
                src = bass.AP(tensor=bias_rows.tensor, offset=bias_rows.offset + 127 + 384 * g, ap=[[1152, 16], [-1, P], [1, 256]])
                act.dma_start(bias_mat[:, :, 256 * g:256 * (g + 1)], src).then_inc(b_skewed, 16)
            src = bass.AP(tensor=bias_rows.tensor, offset=bias_rows.offset + 127 + 768, ap=[[1152, 16], [-1, 64], [1, 64]])
            act.dma_start(bias_mat2, src).then_inc(b_skewed, 16)
            act.wait_ge(b_skewed, 48)
            stage_end(act, 2)

            act.sem_inc(g_evac[0], 1)
            act.sem_inc(g_evac[1], 1)
            with act.Fori(0, HP) as hp:
                act.wait_ge(c_free, 3 * hp + 1)
                pair = bass.ds(2 * hp, 2)
                act.dma_start(BIAS[:, :, 0:512], bias_mat[pair].rearrange("h p c -> p h c")).then_inc(a_bias, 16)
                for half in range(2):
                    act.dma_start(BIAS[64 * half:64 * half + 64, :, 512 + 64 * half:576 + 64 * half],
                                  bias_mat2[pair].rearrange("h p c -> p h c")).then_inc(a_bias, 16)
                for j in range(L1_PER_HP):
                    if j in (3, 6):
                        act.wait_ge(c_free, 3 * hp + (j // 3 + 1))
                    act.wait_ge(slot_used, L1_PER_HP * hp + j + 3)
                    if SLOT_OF[j] == "gate":
                        nc.scalar.activation(GATE[:, :], psum[:, 0:2, :].rearrange("p a c -> p (a c)"),
                                             ACT.Tanh, scale=0.5).then_inc(g_gate, 1)
                    else:
                        evac_qkv(j).then_inc(g_evac[j % 2], 1)
                for n in range(NU):
                    g, u = UNITS[n]
                    nk = len(key_tiles(g, u))
                    if n % 8 == 0:
                        act.wait_ge(v_turned, 6 * hp + 2 * g + 1)
                        nc.scalar.copy(VROW[:, 0:4, :].rearrange("p a c -> p (a c)"), psum[:, 5, :]).then_inc(v_rows[0], 1)
                    act.wait_ge(u_negmax, NU * hp + n + 1)
                    for h in range(2):
                        lg = LOG[:, n % 2, h * 256:h * 256 + P * nk]
                        nc.scalar.activation(lg, lg, ACT.Exp, bias=STAT[:, n % 2, 4 + h:5 + h],
                                             accum_out=STAT[:, n % 2, h:h + 1]).then_inc(u_probs, 1)
                    act.wait_ge(u_probs, 2 * NU * hp + 2 * n + 2)
                    nc.scalar.copy(WIDE[:, n % 2, :].rearrange("p (a c) -> p a c", a=4),
                                   STAT[:, n % 2, 0:4].rearrange("p (a o) -> p a o", o=1).to_broadcast([P, 4, 64])
                                   ).then_inc(u_wide, 1)
                    act.wait_ge(u_turned, NU * hp + n + 1)
                    if n >= 2:
                        act.wait_ge(u_out, NU * hp + n - 1)
                    nc.scalar.copy(PT[:, n % 2, :].rearrange("p (h c) -> p h c", h=2)[:, :, 0:nk * P],
                                   psum[:, 5 + n % 2, :].rearrange("p (h c) -> p h c", h=2)[:, :, 0:nk * P]).then_inc(u_pt, 1)
                for i, g in enumerate(MERGE):
                    act.wait_ge(c_diff, 3 * hp + i + 1)
                    nc.scalar.activation(QKV[:, 3 * g + 2], QKV[:, 3 * g + 2], ACT.Exp).then_inc(c_act, 1)
            stage_end(act, 3)
            y_act(act, 0, Y1, True)
            stage_end(act, 4)
            f_act(act, 0, SLOT_F1, HALVES, rows8(x_in), rows8(x1), io["attn_post_norm"][0])
            stage_end(act, 5)
            act.dma_start(T_GAIN[:, 0, :], io["ssm_pre_norm"].rearrange("a (k p) -> p (a k)", p=P),
                          allow_slow_non_contiguous=True).then_inc(const_loaded, 16)
            act.wait_ge(const_loaded, 16 * 4)
            t_act(act, 8, NT, rows8(x1), True, T_GAIN, 0)
            stage_end(act, 6)
            for n in range(8):
                b = n % 2
                act.wait_ge(slot_used, SLOT_U + 2 * KT + KT * (n // 4 + 1) + 2)
                if n >= 2:
                    act.wait_ge(z_stored[b], 16 * (n // 2))
                nc.scalar.activation(F_T2[:, b], ps_tile(n % 4), ACT.Silu).then_inc(z_scaled, 1)
                act.wait_ge(z_scaled, n + 1)
                act.dma_start(rows8(z_rows)(n), F_T2[:, b]).then_inc(z_stored[b], 16)
            for b in range(2):
                act.wait_ge(z_stored[b], 64)
            stage_end(act, 7)
            act.dma_start(Q1.rearrange("p a b c -> p (a b c)"), q_pow).then_inc(q_loaded, 16)
            for gp in range(2):
                act.dma_start(SP_RING[:, gp, 0:256], b_mat[gp]).then_inc(s_loaded[gp % 2], 16)
            for gp in range(G2):
                act.wait_ge(s_turned, gp + 1)
                if gp >= 2:
                    act.wait_ge(s_mul, gp - 1)
                nc.scalar.copy(UT[:, gp % 2], psum[:, gp % 2, 0:256]).then_inc(s_ut, 1)
                if 1 <= gp < G2 - 1:
                    act.wait_ge(s_mul, gp)
                    act.dma_start(SP_RING[:, (gp + 1) % 2, 0:256], b_mat[gp + 1]).then_inc(s_loaded[(gp + 1) % 2], 16)

            def load_cm(gp):
                act.dma_start(SP_RING[:, gp % 2, 0:256], m_mat[gp]).then_inc(s_loaded[gp % 2], 16)
                act.dma_start(SP_RING[:, gp % 2, 256:512], c_mat[gp]).then_inc(s_loaded[gp % 2], 16)

            act.wait_ge(s_mul, G2)
            load_cm(0)
            load_cm(1)
            for gp in range(G2):
                n = G2 + gp
                act.wait_ge(s_turned, n + 1)
                if gp >= 2:
                    act.wait_ge(s_mul, n - 1)
                nc.scalar.copy(UT[:, gp % 2], psum[:, n % 2, 0:256]).then_inc(s_ut, 1)
                if 1 <= gp < G2 - 1:
                    act.wait_ge(s_mul, n)
                    load_cm(gp + 1)
            act.wait_ge(s_out, 2 * G2)
            for t in range(NT):
                nc.scalar.activation(YR[:, t], YR[:, t], ACT.Gelu_apprx_tanh).then_inc(e_gelu, 1)
            stage_end(act, 8)
            x_act(act, 0, NT, False)
            stage_end(act, 9)
            act.dma_start(F_GAIN, spread_rows(io["ssm_b_glu"][0])).then_inc(h_const, 16)
            for n in range(2):
                act.dma_start(F_X[:, n], rows8(z_rows)(n)).then_inc(h_z[n], 16)
            for n in range(8):
                act.wait_ge(h_sum, n + 1)
                nc.scalar.activation(F_T[:, n % 2], F_T[:, n % 2], ACT.Sigmoid).then_inc(h_gate, 1)
                if n + 2 < 8:
                    act.wait_ge(h_done, n + 1)
                    act.dma_start(F_X[:, n % 2], rows8(z_rows)(n + 2)).then_inc(h_z[n % 2], 16)
            stage_end(act, 10)
            x_act(act, 8, NT, True)
            stage_end(act, 11)
            f_act(act, 8, SLOT_U + 6 * KT, HALVES, rows(x1), rows(x2), io["ssm_post_norm"][0])
            stage_end(act, 12)
            for i, name in enumerate(("c_2", "c_ctx_2")):
                v = io[name].rearrange("b d -> (b d)") if i == 0 else io[name]
                act.dma_start(c_cols[:, :, i], v.rearrange("(k p) -> p k", p=P), allow_slow_non_contiguous=True).then_inc(m_c, 16)
            for l in range(2):
                hybrid_act(act, l)

        @block.vector
        def _(dve):
            V = nc.vector
            n_link = [0]

            def kl(ins, n=1):
                n_link[0] += 1
                ins.then_inc(k_chain, 1)
                dve.wait_ge(k_chain, n_link[0])

            def exp_of(dst, src, a, b, c):
                kl(V.tensor_scalar(src, src, 87.0, -87.0, ALU.min, ALU.max))
                kl(V.tensor_scalar(a, src, 1.0 / math.log(2.0), MAGIC, ALU.mult, ALU.add))
                kl(V.tensor_scalar(a, a, MAGIC, None, ALU.subtract))
                kl(V.scalar_tensor_tensor(b, a, -LN2_HI, src, ALU.mult, ALU.add))
                kl(V.scalar_tensor_tensor(b, a, -LN2_LO, b, ALU.mult, ALU.add))
                kl(V.tensor_scalar(dst, b, 1.0 / 5040, 1.0 / 720, ALU.mult, ALU.add))
                for f in (1 / 120, 1 / 24, 1 / 6, 0.5, 1.0, 1.0):
                    kl(V.tensor_tensor(dst, dst, b, ALU.mult))
                    kl(V.tensor_scalar(dst, dst, f, None, ALU.add))
                kl(V.tensor_scalar(c.bitcast(I32), a, 127.0, None, ALU.add))
                kl(V.tensor_scalar(c.bitcast(I32), c.bitcast(I32), 23, None, ALU.logical_shift_left))
                kl(V.tensor_tensor(dst, dst, c, ALU.mult))

            kl(V.memset(KZ, 0.0))
            dve.wait_ge(k_load, 16 * K_LOADS)
            A_ = lambda i: KA[:, i]
            AR, AI, LD, DT, ER = A_(0), A_(1), A_(2), A_(3), A_(4)
            exp_of(DT, LD, A_(10), A_(11), A_(12))
            kl(V.tensor_tensor(A_(13), DT, AR, ALU.mult))
            exp_of(ER, A_(13), A_(10), A_(11), A_(12))
            kl(V.tensor_tensor(A_(5), DT, AI, ALU.mult))
            for i, shift in ((0, 0.0), (1, 0.25)):
                kl(V.tensor_scalar(A_(10), A_(5), 1.0 / (2 * math.pi), shift, ALU.mult, ALU.add))
                kl(V.tensor_scalar(A_(10), A_(10), MAGIC, None, ALU.add))
                kl(V.tensor_scalar(A_(10), A_(10), MAGIC, None, ALU.subtract))
                kl(V.scalar_tensor_tensor(A_(11), A_(10), -TWO_PI_1, A_(5), ALU.mult, ALU.add))
                kl(V.scalar_tensor_tensor(A_(11), A_(10), -TWO_PI_2, A_(11), ALU.mult, ALU.add))
                kl(V.scalar_tensor_tensor(A_(11), A_(10), -TWO_PI_3, A_(11), ALU.mult, ALU.add))
                kl(V.tensor_scalar(A_(11), A_(11), 2 * math.pi * shift, PI_BELOW, ALU.add, ALU.min))
                kl(V.tensor_scalar(A_(6 + i), A_(11), -PI_BELOW, None, ALU.max))
            V.tensor_copy(A_(14), A_(5)).then_inc(k_arg, 1)
            dve.wait_ge(k_trig, 1)
            PR, PI = KP[:, 0], KP[:, 1]
            kl(V.memset(PR[:, 0], 1.0))
            kl(V.memset(PI[:, 0], 0.0))
            kl(V.tensor_tensor(PR[:, 1], ER, A_(9), ALU.mult))
            kl(V.tensor_tensor(PI[:, 1], ER, A_(8), ALU.mult))

            def cmul(dr, di, ar, ai, br, bi, t, u, bsign=1):
                kl(V.tensor_tensor(t, ar, br, ALU.mult))
                kl(V.tensor_tensor(u, ai, bi, ALU.mult))
                kl(V.tensor_tensor(dr, t, u, ALU.subtract))
                kl(V.tensor_tensor(t, ar, bi, ALU.mult))
                kl(V.tensor_tensor(u, ai, br, ALU.mult))
                kl(V.tensor_tensor(di, t, u, ALU.add))

            def over(v, n):
                return v.rearrange("p (o g) -> p o g", o=1).to_broadcast([P, n, 32])

            ta, tb = KT1.rearrange("p a b -> p (a b)")[:, 0:256], KT1.rearrange("p a b -> p (a b)")[:, 256:512]
            tv = lambda v, n: v[:, 0:32 * n].rearrange("p (n g) -> p n g", g=32)
            for have in (1, 2, 4):
                cmul(PR[:, have + 1:2 * have + 1], PI[:, have + 1:2 * have + 1], PR[:, 1:have + 1], PI[:, 1:have + 1],
                     over(PR[:, have], have), over(PI[:, have], have), tv(ta, have), tv(tb, have))
            kl(V.tensor_copy(KQ[:, :, 0], KP[:, :, 8]))
            for have in (1, 2, 4, 8):
                QR, QI = KQ[:, 0], KQ[:, 1]
                cmul(QR[:, have:2 * have], QI[:, have:2 * have], QR[:, 0:have], QI[:, 0:have],
                     over(QR[:, have - 1], have), over(QI[:, have - 1], have), tv(ta, have), tv(tb, have))
            kl(V.tensor_scalar(A_(10), PR[:, 1], -1.0, None, ALU.add))
            kl(V.tensor_tensor(A_(11), AR, AR, ALU.mult))
            kl(V.tensor_tensor(A_(12), AI, AI, ALU.mult))
            kl(V.tensor_tensor(A_(11), A_(11), A_(12), ALU.add))
            kl(V.reciprocal(A_(11), A_(11)))
            kl(V.tensor_tensor(A_(12), A_(10), AR, ALU.mult))
            kl(V.tensor_tensor(A_(13), PI[:, 1], AI, ALU.mult))
            kl(V.tensor_tensor(A_(12), A_(12), A_(13), ALU.add))
            kl(V.tensor_tensor(A_(15), A_(12), A_(11), ALU.mult))
            kl(V.tensor_tensor(A_(12), PI[:, 1], AR, ALU.mult))
            kl(V.tensor_tensor(A_(13), A_(10), AI, ALU.mult))
            kl(V.tensor_tensor(A_(12), A_(12), A_(13), ALU.subtract))
            kl(V.tensor_tensor(A_(16), A_(12), A_(11), ALU.mult))

            def deep(v):
                return v.rearrange("p (g o) -> p g o", o=1).to_broadcast([P, 32, 16])

            kl(V.tensor_tensor(KBB[:, 0], KB[:, 0], deep(A_(15)), ALU.mult))
            kl(V.tensor_tensor(KT1, KB[:, 1], deep(A_(16)), ALU.mult))
            kl(V.tensor_tensor(KBB[:, 0], KBB[:, 0], KT1, ALU.subtract))
            kl(V.tensor_tensor(KBB[:, 1], KB[:, 1], deep(A_(15)), ALU.mult))
            kl(V.tensor_tensor(KT1, KB[:, 0], deep(A_(16)), ALU.mult))
            kl(V.tensor_tensor(KBB[:, 1], KBB[:, 1], KT1, ALU.add))
            for ri in range(2):
                if ri == 1:
                    dve.wait_ge(k_bt, 8)
                for s_ in range(8):
                    dst = KBP[:, :, s_, :]
                    kl(V.tensor_tensor(dst, KBB[:, ri], deep(PR[:, s_]), ALU.mult))
                    kl(V.tensor_tensor(KT1, KBB[:, 1 - ri], deep(PI[:, s_]), ALU.mult))
                    V.tensor_tensor(dst, dst, KT1, ALU.subtract if ri == 0 else ALU.add).then_inc(k_part, 1)
                    dve.wait_ge(k_part, 8 * ri + s_ + 1)
                V.tensor_copy(A_(17), A_(16)).then_inc(k_b, 1)
            dve.wait_ge(k_c, 8)
            for t in range(9):
                cr, ci = KCP[:, 0, :, 16 * t:16 * t + 16], KCP[:, 1, :, 16 * t:16 * t + 16]
                kl(V.tensor_tensor(cr, KC[:, 0], deep(PR[:, t]), ALU.mult))
                kl(V.tensor_tensor(KT1, KC[:, 1], deep(PI[:, t]), ALU.mult))
                kl(V.tensor_tensor(cr, cr, KT1, ALU.subtract))
                kl(V.tensor_tensor(ci, KC[:, 0], deep(PI[:, t]), ALU.mult))
                kl(V.tensor_tensor(KT1, KC[:, 1], deep(PR[:, t]), ALU.mult))
                kl(V.scalar_tensor_tensor(ci, ci, -1.0, KT1, ALU.mult, ALU.subtract))
            V.tensor_copy(A_(17), A_(16)).then_inc(k_cp, 1)
            kl(V.tensor_tensor(KD[0:16], KD[0:16], ident[0:16, 0:16].rearrange("p (o c) -> p o c", o=1).to_broadcast([16, 64, 16]),
                               ALU.mult))
            for bt in range(8):
                dve.wait_ge(k_conv, bt + 1)
                if bt >= 2:
                    dve.wait_ge(k_kst[bt % 2], 32 * (bt // 2))
                V.tensor_copy(KK[0:16, bt % 2], psum[0:16, 2 * (bt % 2):2 * (bt % 2) + 2, :]).then_inc(k_kk, 1)
                dve.wait_ge(k_kk, 2 * bt + 1)
                at0 = KK[0:16, bt % 2].rearrange("p g (a k) -> p g a k", a=4)[:, :, :, 0:16]
                V.tensor_tensor(at0, at0, KD[0:16, 8 * bt:8 * bt + 8].rearrange("p (a g) c -> p g a c", g=2),
                                ALU.add).then_inc(k_kk, 1)
            stage_end(dve, 1)

            nc.vector.memset(relb[32:33, :], NEG).then_inc(b_copied, 1)
            nc.vector.memset(T_GAIN[:, 1, :], 0.0).then_inc(b_copied, 1)
            dve.wait_ge(b_spread, 1)
            nc.vector.tensor_copy(spread[0:16, :, :], psum[0:16, 4:7, 0:384]).then_inc(b_copied, 1)
            t_dve(dve, 0, NT, True, T_GAIN, 0)
            stage_end(dve, 2)

            nc.vector.memset(BIAS[0:64, :, 576:640], NEG).then_inc(c_zero, 1)
            nc.vector.memset(BIAS[64:128, :, 512:576], NEG).then_inc(a_neg, 1)
            dve.wait_ge(a_neg, 1)
            dve.wait_ge(c_zero, 1)
            dve.sem_inc(c_free, 3)
            with dve.Fori(0, HP) as hp:
                dve.wait_ge(g_gate, hp + 1)
                nc.vector.scalar_tensor_tensor(GATE[:, :], GATE[:, :], 1.0,
                                               psum[:, 0:2, :].rearrange("p a c -> p (a c)"),
                                               ALU.add, ALU.mult).then_inc(g_evac[0], 1)
                dve.wait_ge(a_bias, 48 * hp + 48)
                for n in range(NU):
                    g, u = UNITS[n]
                    nk = len(key_tiles(g, u))
                    if n % 8 == 0:
                        dve.wait_ge(v_turned, 6 * hp + 2 * g + 2)
                        nc.vector.tensor_copy(VROW[:, 4:8, :].rearrange("p a c -> p (a c)"),
                                              psum[:, 6, :]).then_inc(v_rows[1], 1)

                    def logits(n):
                        g, u = UNITS[n]
                        nk = len(key_tiles(g, u))
                        dve.wait_ge(u_scores, NU * hp + n + 1)
                        if n >= 2:
                            dve.wait_ge(u_wide, NU * hp + n - 1)
                            dve.wait_ge(u_turned, NU * hp + n - 1)
                        nc.vector.memset(STAT[:, n % 2, 6:7], 0.0)
                        for h in range(2):
                            nc.vector.tensor_tensor_reduce(LOG[:, n % 2, h * 256:h * 256 + P * nk],
                                                           psum[:, 2 * (n % 2) + h, 0:P * nk],
                                                           BIAS[:, h, bias_cols(g, u)], 1.0, -3e38, ALU.add, ALU.max,
                                                           accum_out=STAT[:, n % 2, 2 + h:3 + h]).then_inc(u_logits, 1)
                        dve.wait_ge(u_logits, 2 * NU * hp + 2 * n + 2)
                        nc.vector.tensor_scalar(STAT[:, n % 2, 4:6], STAT[:, n % 2, 2:4], -1.0, None,
                                                ALU.mult).then_inc(u_negmax, 1)

                    if n % 8 == 0:
                        logits(n)
                    if n % 8 < 7:
                        logits(n + 1)
                    dve.wait_ge(u_out, NU * hp + n + 1)
                    nc.vector.tensor_copy(QKV[:, 3 * g:3 * g + 3, u * P:(u + 1) * P],
                                          psum[:, OB(n), 0:3 * P].rearrange("p (a c) -> p a c", a=3)).then_inc(u_evac, 1)
                dve.wait_ge(u_evac, NU * hp + NU)
                chain = [0]

                def link(ins):
                    chain[0] += 1
                    ins.then_inc(c_dve, 1)
                    dve.wait_ge(c_dve, 15 * hp + chain[0])

                tt = nc.vector.tensor_tensor
                top = PT[:, :, :].rearrange("p a c -> p (a c)")
                split_t = lambda v, g: v if g == 0 else v.rearrange("p (m r) -> p m r", r=GROUPS[g][1])
                link(tt(split_t(top, 1), split_t(QKV[:, 2], 1), scatter(QKV[:, 5], 1), ALU.max))
                link(tt(split_t(top, 2), split_t(top, 2), scatter(QKV[:, 8], 2), ALU.max))
                for g in MERGE:
                    m = scatter(QKV[:, 3 * g + 2], g)
                    tt(m, m, split_t(top, g), ALU.subtract).then_inc(c_diff, 1)
                for i, g in enumerate(MERGE):
                    dve.wait_ge(c_act, 3 * hp + i + 1)
                    for i in (0, 1):
                        link(tt(QKV[:, 3 * g + i], QKV[:, 3 * g + i], QKV[:, 3 * g + 2], ALU.mult))
                    if g > 0:
                        for i in (0, 1):
                            link(tt(split_t(QKV[:, i], g), split_t(QKV[:, i], g), scatter(QKV[:, 3 * g + i], g), ALU.add))
                        dve.sem_inc(c_free, 1)
                link(nc.vector.reciprocal(top, QKV[:, 1]))
                link(tt(QKV[:, 0], QKV[:, 0], top, ALU.mult))
                link(nc.vector.scalar_tensor_tensor(Y1[:, bass.ds(hp, 1), :].rearrange("p a c -> p (a c)"),
                                                    QKV[:, 0], 0.5, GATE[:, :], ALU.mult, ALU.mult))
                dve.sem_inc(c_free, 1)
            stage_end(dve, 3)
            y_dve(dve, 0, Y1, True)
            stage_end(dve, 4)
            f_dve(dve, 0, HALVES, 1)
            stage_end(dve, 5)
            V.memset(T_GAIN[:, 1, :], 0.0).then_inc(b_copied, 1)
            t_dve(dve, 8, NT, True, T_GAIN, 0)
            stage_end(dve, 6)
            for n in range(8):
                dve.wait_ge(slot_used, SLOT_U + KT * (n // 4 + 1) + 2)
                V.tensor_copy(U[:, :, (7 - n) * 16:(8 - n) * 16],
                              ps_tile(n % 4).rearrange("p (g c) -> p g c", g=64)).then_inc(u_copied, 1)
            stage_end(dve, 7)
            V.memset(ST[:, :, :, 0:1], 0.0).then_inc(s_zero, 1)
            for gp in range(G2):
                dve.wait_ge(s_mul, gp + 1)
                V.tensor_copy(ST[:, gp, :, 1:129], psum[:, 2 + gp % 2, 0:256].rearrange("p (r c) -> p r c", r=2)).then_inc(s_out, 1)
            n_q = [0]

            def ql(ins):
                n_q[0] += 1
                ins.then_inc(q_dve, 1)
                dve.wait_ge(q_dve, n_q[0])

            dve.wait_ge(q_loaded, 16)
            q = Q1.rearrange("p a b c -> p (a b c)").rearrange("p (r j g) -> p r g j", r=2, j=16)
            for r in range(2):
                ql(V.tensor_copy(QRR[:, :, r], q[:, 0]))
            ql(V.tensor_scalar(QIS[:, :, 0], q[:, 1], -1.0, None, ALU.mult))
            ql(V.tensor_copy(QIS[:, :, 1], q[:, 1]))
            dve.wait_ge(s_zero, 1)
            dve.wait_ge(s_out, G2)

            def swapped(v):
                ap = [list(x) for x in v.ap]
                off = v.offset + ap[2][0] * (ap[2][1] - 1)
                ap[2][0] = -ap[2][0]
                return bass.AP(tensor=v.tensor, offset=off, ap=ap)

            def advance(x, prev, j, width):
                qr = QRR[:, :, :, j - 1:j].to_broadcast([P, 32, 2, width])
                qi = QIS[:, :, :, j - 1:j].to_broadcast([P, 32, 2, width])
                t1 = Q1.rearrange("p a b c -> p (a b c)")[:, 0:64 * width].rearrange("p (a b c) -> p a b c", a=32, b=2)
                t2 = Q2.rearrange("p a b c -> p (a b c)")[:, 0:64 * width].rearrange("p (a b c) -> p a b c", a=32, b=2)
                ql(V.tensor_tensor(t1, prev, qr, ALU.mult))
                ql(V.tensor_tensor(t2, swapped(prev), qi, ALU.mult))
                ql(V.tensor_tensor(x, x, t1, ALU.add))
                ql(V.tensor_tensor(x, x, t2, ALU.add))

            for j in range(1, 16):
                advance(ST[:, :, :, 1 + j:129:16], ST[:, :, :, j:128:16], 1, 8)
            for b in range(1, 8):
                advance(ST[:, :, :, 16 * b + 16:16 * b + 17], ST[:, :, :, 16 * b:16 * b + 1], 16, 1)
            for b in range(1, 8):
                x = ST[:, :, :, 16 * b + 1:16 * b + 16]
                last = ST[:, :, :, 16 * b:16 * b + 1].to_broadcast([P, 32, 2, 15])
                last_s = swapped(ST[:, :, :, 16 * b:16 * b + 1].to_broadcast([P, 32, 2, 15]))
                t1, t2 = Q1[:, :, :, 0:15], Q2[:, :, :, 0:15]
                ql(V.tensor_tensor(t1, last, QRR[:, :, :, 0:15], ALU.mult))
                ql(V.tensor_tensor(t2, last_s, QIS[:, :, :, 0:15], ALU.mult))
                ql(V.tensor_tensor(x, x, t1, ALU.add))
                ql(V.tensor_tensor(x, x, t2, ALU.add))
            assert n_q[0] == Q_OPS, n_q[0]
            for gp in range(G2):
                n = G2 + gp
                dve.wait_ge(s_mul, n + 1)
                b0 = 4 + 2 * (gp % 2)
                dst = YR[:, :, 32 * gp:32 * gp + 32].rearrange("p t (g c) -> p g t c", g=2)
                for g2 in range(2):
                    ins = V.tensor_copy(dst[:, g2], psum[:, b0 + g2, 0:P].rearrange("p (t c) -> p t c", t=8))
                ins.then_inc(s_out, 1)
            stage_end(dve, 8)
            x_dve(dve, 0, NT, False)
            stage_end(dve, 9)
            dve.wait_ge(h_const, 16)
            for n in range(8):
                b = n % 2
                dve.wait_ge(slot_used, SLOT_U + 4 * KT + KT * (n // 4 + 1) + 2)
                if n >= 2:
                    dve.wait_ge(h_part, n - 1)
                V.tensor_tensor(F_T[:, b], ps_tile(n % 4), F_GAIN, ALU.add).then_inc(h_sum, 1)
                dve.wait_ge(h_gate, n + 1)
                V.tensor_tensor(F_T[:, b], F_T[:, b], YR[:, n], ALU.mult).then_inc(h_part, 1)
                dve.wait_ge(h_part, n + 1)
                dve.wait_ge(h_z[b], 16 * (n // 2 + 1))
                V.tensor_tensor(YR[:, n], F_T[:, b], F_X[:, b], ALU.mult).then_inc(h_done, 1)
            stage_end(dve, 10)
            x_dve(dve, 8, NT, True)
            stage_end(dve, 11)
            f_dve(dve, 8, HALVES, 2)
            stage_end(dve, 12)
            for l in range(2):
                hybrid_dve(dve, l)


NAMES = (
    "x", "rel_bias", "attn_pre_norm", "attn_w_in", "attn_w_out", "attn_post_norm",
    "ssm_pre_norm", "ssm_w_in", "ssm_a_re", "ssm_a_im", "ssm_log_dt", "ssm_b_re",
    "ssm_b_im", "ssm_c_re", "ssm_c_im", "ssm_d", "ssm_w_glu", "ssm_b_glu",
    "ssm_w_out", "ssm_post_norm", "c_2", "ctx_2", "c_ctx_2", "w_mod_2",
    "b_mod_2", "w_in_2", "conv_w_2", "conv_b_2", "ret_decay_2", "na_rpb_2",
    "w_out_2", "ln_g_2", "ln_b_2",
)


def kernel(**inputs):
    import numpy as _np
    import concourse.bacc as _bacc
    from concourse import mybir as _mybir
    from concourse.bass_utils import run_bass_kernel_spmd as _run

    nc = _bacc.Bacc("TRN2", target_bir_lowering=False, num_devices=1)
    arrays, io = {}, {}
    for name in NAMES:
        a = _np.ascontiguousarray(inputs[name])
        arrays[f"in_{name}"] = a
        io[name] = nc.dram_tensor(f"in_{name}", a.shape, _mybir.dt.from_np(a.dtype), kind="ExternalInput").ap()
    for name, a in constants().items():
        arrays[name] = a
        io[name] = nc.dram_tensor(name, a.shape, _mybir.dt.from_np(a.dtype), kind="ExternalInput").ap()
    out = nc.dram_tensor("out_0_dram", (1, S, D), F32, kind="ExternalOutput").ap()
    build(nc, io, out)
    r = _run(nc, [arrays], core_ids=[0])
    return r.results[0]["out_0_dram"]
```
